# Optimizing a Trainium2 kernel written in Bass

```python
import jax, jax.numpy as jnp
from jax import lax
import numpy as np
import math

D_MODEL = 1024
BATCH = 1
SEQ = 256
DEPTH = 4

N_MIXERS = 3
N_A = (DEPTH + 2) // 3
N_B = (DEPTH + 1) // 3
N_C = DEPTH // 3
EPS = 1e-6

GM_CHUNK = 128
GM_GROUPS = 8
GM_INNER = 2 * D_MODEL
GM_GROUP_DIM = GM_INNER // GM_GROUPS

MLA_HEADS = 8
MLA_Q_RANK = D_MODEL // 4
MLA_KV_RANK = D_MODEL // 8
MLA_NOPE = 128
MLA_ROPE = 64
MLA_V = 128
ROPE_THETA = 10000.0
ATTN_BLOCK = 128

HG_HEADS = 8
HG_DK = 128
HG_DV = D_MODEL // HG_HEADS
HG_CHUNK = 64

FF_DIM = 2816
CONV_W = 3


def rmsnorm(x, g):
    xf = x.astype(jnp.float32)
    y = xf * lax.rsqrt(jnp.mean(xf * xf, axis=-1, keepdims=True) + EPS)
    return (y * g.astype(jnp.float32)).astype(x.dtype)

def layernorm(x, g, b):
    xf = x.astype(jnp.float32)
    mu = jnp.mean(xf, axis=-1, keepdims=True)
    var = jnp.mean(jnp.square(xf - mu), axis=-1, keepdims=True)
    y = (xf - mu) * lax.rsqrt(var + EPS) * g.astype(jnp.float32) + b.astype(jnp.float32)
    return y.astype(x.dtype)

def modulate(h, shift, scale):
    return h * (1.0 + scale[:, None, :]) + shift[:, None, :]

def rope_tables(positions):
    inv_freq = ROPE_THETA ** (-jnp.arange(0, MLA_ROPE, 2, dtype=jnp.float32) / MLA_ROPE)
    ang = positions.astype(jnp.float32)[..., None] * inv_freq
    return jnp.cos(ang)[:, :, None, :], jnp.sin(ang)[:, :, None, :]

def apply_rope(x, cos, sin):
    x1, x2 = jnp.split(x, 2, axis=-1)
    cos = cos.astype(x.dtype)
    sin = sin.astype(x.dtype)
    return jnp.concatenate([x1 * cos - x2 * sin, x2 * cos + x1 * sin], axis=-1)

def gmlp_mixer(h, w_in, ln_g, ln_b, w_s, b_s, w_out):
    B, S, _ = h.shape
    z = jax.nn.gelu(h @ w_in)
    u, v = jnp.split(z, 2, axis=-1)
    v = layernorm(v, ln_g, ln_b)
    n = S // GM_CHUNK
    v = v.reshape(B, n, GM_CHUNK, GM_GROUPS, GM_GROUP_DIM)
    mask = jnp.tril(jnp.ones((GM_CHUNK, GM_CHUNK), dtype=bool))
    ws = jnp.where(mask[None], w_s, jnp.zeros_like(w_s))
    sv = jnp.einsum('gts,bnsgd->bntgd', ws, v) + b_s.T[None, None, :, :, None]
    y = u * sv.reshape(B, S, GM_INNER)
    return y @ w_out

def causal_block_attention(q, k, v, scale):
    B, S, H, Dk = q.shape
    nb = S // ATTN_BLOCK
    qb = q.reshape(B, nb, ATTN_BLOCK, H, Dk).transpose(1, 0, 2, 3, 4)
    kpos = jnp.arange(S)

    def one_block(args):
        qi, bi = args
        s = jnp.einsum('bqhd,bkhd->bhqk', qi, k).astype(jnp.float32) * scale
        qpos = bi * ATTN_BLOCK + jnp.arange(ATTN_BLOCK)
        s = jnp.where(kpos[None, :] <= qpos[:, None], s, -jnp.inf)
        p = jax.nn.softmax(s, axis=-1).astype(v.dtype)
        return jnp.einsum('bhqk,bkhd->bqhd', p, v)

    o = lax.map(one_block, (qb, jnp.arange(nb)))
    return o.transpose(1, 0, 2, 3, 4).reshape(B, S, H, v.shape[-1])

def mla_mixer(h, cos, sin, w_a, q_norm_g, kv_norm_g, w_qb, w_kvb, w_o):
    B, S, _ = h.shape
    a = h @ w_a
    cq = a[..., :MLA_Q_RANK]
    ckv = a[..., MLA_Q_RANK:MLA_Q_RANK + MLA_KV_RANK]
    k_rope = a[..., MLA_Q_RANK + MLA_KV_RANK:]
    q = (rmsnorm(cq, q_norm_g) @ w_qb).reshape(B, S, MLA_HEADS, MLA_NOPE + MLA_ROPE)
    q_nope, q_rope = q[..., :MLA_NOPE], q[..., MLA_NOPE:]
    kv = (rmsnorm(ckv, kv_norm_g) @ w_kvb).reshape(B, S, MLA_HEADS, MLA_NOPE + MLA_V)
    k_nope, v = kv[..., :MLA_NOPE], kv[..., MLA_NOPE:]
    q_rope = apply_rope(q_rope, cos, sin)
    k_rope = apply_rope(k_rope[:, :, None, :], cos, sin)
    k_rope = jnp.broadcast_to(k_rope, (B, S, MLA_HEADS, MLA_ROPE))
    q = jnp.concatenate([q_nope, q_rope], axis=-1)
    k = jnp.concatenate([k_nope, k_rope], axis=-1)
    o = causal_block_attention(q, k, v, (MLA_NOPE + MLA_ROPE) ** -0.5)
    return o.reshape(B, S, MLA_HEADS * MLA_V) @ w_o

def hgrn_lower_bounds(lb_param):
    p = jax.nn.softmax(lb_param.astype(jnp.float32), axis=0)
    return jnp.cumsum(p, axis=0) - p[0:1]

def chunked_gated_recurrence(q, k, v, log_f):
    B, S, H, DK = q.shape
    DV = v.shape[-1]
    C = HG_CHUNK
    n = S // C

    def to_chunks(t):
        return t.astype(jnp.float32).reshape(B, n, C, H, t.shape[-1]).transpose(1, 0, 3, 2, 4)

    qc, kc, vc, gc = to_chunks(q), to_chunks(k), to_chunks(v), to_chunks(log_f)
    causal = jnp.tril(jnp.ones((C, C), dtype=bool))[:, :, None]

    def step(state, inp):
        qi, ki, vi, gi = inp
        bcum = jnp.cumsum(gi, axis=2)
        rel = bcum[:, :, :, None, :] - bcum[:, :, None, :, :]
        decay = jnp.exp(jnp.where(causal, rel, -jnp.inf))
        attn = jnp.einsum('bhtk,bhtsk,bhsk->bhts', qi, decay, ki)
        o = jnp.einsum('bhts,bhsv->bhtv', attn, vi) + jnp.einsum('bhtk,bhkv->bhtv', qi * jnp.exp(bcum), state)
        blast = bcum[:, :, -1:, :]
        new_state = jnp.exp(blast[:, :, 0, :])[..., None] * state + jnp.einsum('bhsk,bhsv->bhkv', ki * jnp.exp(blast - bcum), vi)
        return new_state, o

    state0 = jnp.zeros((B, H, DK, DV), jnp.float32)
    _, o = lax.scan(step, state0, (qc, kc, vc, gc))
    return o.transpose(1, 0, 3, 2, 4).reshape(B, S, H, DV).astype(v.dtype)

def hgrn2_mixer(h, lb, w_in, norm_g, w_o):
    B, S, _ = h.shape
    nk = HG_HEADS * HG_DK
    nv = HG_HEADS * HG_DV
    proj = h @ w_in
    q = proj[..., :nk]
    fl = proj[..., nk:2 * nk]
    i = proj[..., 2 * nk:2 * nk + nv]
    g = proj[..., 2 * nk + nv:]
    f = lb + (1.0 - lb) * jax.nn.sigmoid(fl.astype(jnp.float32))
    log_f = jnp.log(f)
    k = 1.0 - f
    o = chunked_gated_recurrence(
        q.reshape(B, S, HG_HEADS, HG_DK), k.reshape(B, S, HG_HEADS, HG_DK),
        i.reshape(B, S, HG_HEADS, HG_DV), log_f.reshape(B, S, HG_HEADS, HG_DK))
    o = rmsnorm(o, norm_g).reshape(B, S, nv) * jax.nn.silu(g)
    return o @ w_o

def conv_ffn(h, w_up, conv_w, conv_b, w_down):
    S = h.shape[1]
    a = h @ w_up
    pad = jnp.pad(a, ((0, 0), (CONV_W - 1, 0), (0, 0)))
    y = conv_b
    for j in range(CONV_W):
        y = y + conv_w[j] * pad[:, j:j + S, :]
    gate, val = jnp.split(y, 2, axis=-1)
    return (jax.nn.silu(gate) * val) @ w_down

def first_inputs(seed: int = 0) -> dict:
    key = jax.random.key(seed)
    ks = jax.random.split(key, 32)
    f32 = jnp.float32

    def nrm(k, shape, scale):
        return jax.random.normal(k, shape, f32) * scale

    D = D_MODEL
    x = nrm(ks[0], (BATCH, SEQ, D), 1.0)
    c = nrm(ks[1], (BATCH, D), 1.0)
    offset = jax.random.randint(ks[2], (BATCH, 1), 0, 1024, dtype=jnp.int32)
    positions = offset + jnp.arange(SEQ, dtype=jnp.int32)[None, :]
    ada_w = nrm(ks[3], (DEPTH, D, 6 * D), 0.2 * D ** -0.5)
    ada_b = nrm(ks[4], (DEPTH, 6 * D), 0.02)
    mix_norm_g = 1.0 + nrm(ks[5], (DEPTH, D), 0.05)
    ffn_norm_g = 1.0 + nrm(ks[6], (DEPTH, D), 0.05)
    gm_w_in = nrm(ks[7], (N_A, D, 2 * GM_INNER), D ** -0.5)
    gm_ln_g = 1.0 + nrm(ks[8], (N_A, GM_INNER), 0.05)
    gm_ln_b = nrm(ks[9], (N_A, GM_INNER), 0.02)
    gm_w_s = nrm(ks[10], (N_A, GM_GROUPS, GM_CHUNK, GM_CHUNK), GM_CHUNK ** -0.5)
    gm_b_s = 1.0 + nrm(ks[11], (N_A, GM_GROUPS, GM_CHUNK), 0.1)
    gm_w_out = nrm(ks[12], (N_A, GM_INNER, D), GM_INNER ** -0.5)
    mla_w_a = nrm(ks[13], (N_B, D, MLA_Q_RANK + MLA_KV_RANK + MLA_ROPE), D ** -0.5)
    mla_q_norm_g = 1.0 + nrm(ks[14], (N_B, MLA_Q_RANK), 0.05)
    mla_kv_norm_g = 1.0 + nrm(ks[15], (N_B, MLA_KV_RANK), 0.05)
    mla_w_qb = nrm(ks[16], (N_B, MLA_Q_RANK, MLA_HEADS * (MLA_NOPE + MLA_ROPE)), MLA_Q_RANK ** -0.5)
    mla_w_kvb = nrm(ks[17], (N_B, MLA_KV_RANK, MLA_HEADS * (MLA_NOPE + MLA_V)), MLA_KV_RANK ** -0.5)
    mla_w_o = nrm(ks[18], (N_B, MLA_HEADS * MLA_V, D), (MLA_HEADS * MLA_V) ** -0.5)
    hg_lb = nrm(ks[19], (DEPTH, HG_HEADS * HG_DK), 0.5)
    hg_w_in = nrm(ks[20], (N_C, D, 2 * HG_HEADS * HG_DK + 2 * HG_HEADS * HG_DV), D ** -0.5)
    hg_norm_g = 1.0 + nrm(ks[21], (N_C, HG_DV), 0.05)
    hg_w_o = nrm(ks[22], (N_C, HG_HEADS * HG_DV, D), (HG_HEADS * HG_DV) ** -0.5)
    ff_w_up = nrm(ks[23], (DEPTH, D, 2 * FF_DIM), D ** -0.5)
    ff_conv_w = nrm(ks[24], (DEPTH, CONV_W, 2 * FF_DIM), CONV_W ** -0.5)
    ff_conv_b = nrm(ks[25], (DEPTH, 2 * FF_DIM), 0.02)
    ff_w_down = nrm(ks[26], (DEPTH, FF_DIM, D), FF_DIM ** -0.5)
    final_g = 1.0 + nrm(ks[27], (D,), 0.05)
    return {'x': x, 'c': c, 'positions': positions, 'ada_w': ada_w, 'ada_b': ada_b,
            'mix_norm_g': mix_norm_g, 'ffn_norm_g': ffn_norm_g,
            'gm_w_in': gm_w_in, 'gm_ln_g': gm_ln_g, 'gm_ln_b': gm_ln_b, 'gm_w_s': gm_w_s,
            'gm_b_s': gm_b_s, 'gm_w_out': gm_w_out,
            'mla_w_a': mla_w_a, 'mla_q_norm_g': mla_q_norm_g, 'mla_kv_norm_g': mla_kv_norm_g,
            'mla_w_qb': mla_w_qb, 'mla_w_kvb': mla_w_kvb, 'mla_w_o': mla_w_o,
            'hg_lb': hg_lb, 'hg_w_in': hg_w_in, 'hg_norm_g': hg_norm_g, 'hg_w_o': hg_w_o,
            'ff_w_up': ff_w_up, 'ff_conv_w': ff_conv_w, 'ff_conv_b': ff_conv_b, 'ff_w_down': ff_w_down,
            'final_g': final_g}

def first_block(x, c, positions, ada_w, ada_b, mix_norm_g, ffn_norm_g,
              gm_w_in, gm_ln_g, gm_ln_b, gm_w_s, gm_b_s, gm_w_out,
              mla_w_a, mla_q_norm_g, mla_kv_norm_g, mla_w_qb, mla_w_kvb, mla_w_o,
              hg_lb, hg_w_in, hg_norm_g, hg_w_o,
              ff_w_up, ff_conv_w, ff_conv_b, ff_w_down, final_g):
    cos, sin = rope_tables(positions)
    lb_all = hgrn_lower_bounds(hg_lb)
    c_act = jax.nn.silu(c)
    for i in range(DEPTH):
        mod = c_act @ ada_w[i] + ada_b[i]
        sh1, sc1, g1, sh2, sc2, g2 = jnp.split(mod, 6, axis=-1)
        h = modulate(rmsnorm(x, mix_norm_g[i]), sh1, sc1)
        kind, j = i % N_MIXERS, i // N_MIXERS
        if kind == 0:
            y = gmlp_mixer(h, gm_w_in[j], gm_ln_g[j], gm_ln_b[j], gm_w_s[j], gm_b_s[j], gm_w_out[j])
        elif kind == 1:
            y = mla_mixer(h, cos, sin, mla_w_a[j], mla_q_norm_g[j], mla_kv_norm_g[j],
                          mla_w_qb[j], mla_w_kvb[j], mla_w_o[j])
        else:
            y = hgrn2_mixer(h, lb_all[i].astype(h.dtype), hg_w_in[j], hg_norm_g[j], hg_w_o[j])
        x = x + (1.0 + g1)[:, None, :] * y
        h = modulate(rmsnorm(x, ffn_norm_g[i]), sh2, sc2)
        x = x + (1.0 + g2)[:, None, :] * conv_ffn(h, ff_w_up[i], ff_conv_w[i], ff_conv_b[i], ff_w_down[i])
    return rmsnorm(x, final_g)


DEPTH_2 = 2

D_MIX = D_MODEL
GROUP_DIM = 64
W_A = D_MIX // 4
W_SSD = D_MIX // 2
W_CONF = D_MIX - W_A - W_SSD
A_CONV = 3
SSD_HEAD_DIM = 64
SSD_HEADS = W_SSD // SSD_HEAD_DIM
SSD_GROUPS = 2
SSD_STATE = 128
SSD_CONV = 4
SSD_CHUNK = 128
SSD_XBC = W_SSD + 2 * SSD_GROUPS * SSD_STATE
CONF_KERNEL = 31
IN_COLS = 3 * W_A + W_SSD + SSD_XBC + SSD_HEADS + 2 * W_CONF
D_FF = ((8 * D_MODEL // 3 + 127) // 128) * 128
N_EXPERTS = 8
TOP_K = 2
D_FF_EXPERT = 7 * D_MODEL // 2
MOE_BLOCK = 128
N_DENSE = (DEPTH_2 + 1) // 2
N_MOE = DEPTH_2 // 2
EPS_2 = 1e-5

_SPLITS = list(np.cumsum([W_A, W_A, W_A, W_SSD, SSD_XBC, SSD_HEADS])[:])


def rmsnorm_2(x, w):
    xf = x.astype(jnp.float32)
    y = xf * lax.rsqrt(jnp.mean(xf * xf, axis=-1, keepdims=True) + EPS_2)
    return (y * w.astype(jnp.float32)).astype(x.dtype)

def layernorm_2(x, g, b):
    xf = x.astype(jnp.float32)
    mu = jnp.mean(xf, axis=-1, keepdims=True)
    var = jnp.mean(jnp.square(xf - mu), axis=-1, keepdims=True)
    y = (xf - mu) * lax.rsqrt(var + EPS_2)
    return (y * g.astype(jnp.float32) + b.astype(jnp.float32)).astype(x.dtype)

def causal_dwconv(u, w, b=None):
    k, c = w.shape
    y = lax.conv_general_dilated(
        u, w[:, None, :].astype(u.dtype), window_strides=(1,), padding=[(k - 1, 0)],
        dimension_numbers=('NWC', 'WIO', 'NWC'), feature_group_count=c)
    return y if b is None else y + b

def ssd_chunked(xh, dt, a, bm, cm):
    bsz, seq = xh.shape[:2]
    nc = seq // SSD_CHUNK
    r = SSD_HEADS // SSD_GROUPS
    f32 = jnp.float32
    xc = xh.reshape(bsz, nc, SSD_CHUNK, SSD_GROUPS, r, SSD_HEAD_DIM).astype(f32)
    dtc = dt.reshape(bsz, nc, SSD_CHUNK, SSD_GROUPS, r)
    bc = bm.reshape(bsz, nc, SSD_CHUNK, SSD_GROUPS, SSD_STATE).astype(f32)
    cc = cm.reshape(bsz, nc, SSD_CHUNK, SSD_GROUPS, SSD_STATE).astype(f32)
    xdt = xc * dtc[..., None]
    a_cum = jnp.cumsum(dtc * a.reshape(SSD_GROUPS, r), axis=2)
    causal = jnp.tril(jnp.ones((SSD_CHUNK, SSD_CHUNK), dtype=bool))
    seg = a_cum[:, :, :, None] - a_cum[:, :, None, :]
    decay_ls = jnp.exp(jnp.where(causal[:, :, None, None], seg, -jnp.inf))
    cb = jnp.einsum('bclgn,bcsgn->bclsg', cc, bc)
    y_diag = jnp.einsum('bclsg,bclsgr,bcsgrp->bclgrp', cb, decay_ls, xdt)
    decay_to_end = jnp.exp(a_cum[:, :, -1:] - a_cum)
    states = jnp.einsum('bclgn,bclgr,bclgrp->bcgrpn', bc, decay_to_end, xdt)
    chunk_decay = jnp.exp(a_cum[:, :, -1])

    def step(h, inp):
        dec, st = inp
        return dec[..., None, None] * h + st, h

    h0 = jnp.zeros_like(states[:, 0])
    _, h_prev = lax.scan(step, h0, (jnp.moveaxis(chunk_decay, 1, 0), jnp.moveaxis(states, 1, 0)))
    h_prev = jnp.moveaxis(h_prev, 0, 1)
    y_off = jnp.einsum('bclgn,bcgrpn,bclgr->bclgrp', cc, h_prev, jnp.exp(a_cum))
    return (y_diag + y_off).reshape(bsz, seq, SSD_HEADS, SSD_HEAD_DIM)

def gated_rmsnorm(y, z, w):
    yz = (y * jax.nn.silu(z)).astype(jnp.float32)
    shp = yz.shape
    yg = yz.reshape(shp[:-1] + (SSD_GROUPS, shp[-1] // SSD_GROUPS))
    yg = yg * lax.rsqrt(jnp.mean(yg * yg, axis=-1, keepdims=True) + EPS_2)
    return (yg.reshape(shp) * w.astype(jnp.float32)).astype(y.dtype)

def hybrid_mixer(h, w_in, conv_a_w, conv_ssd_w, conv_ssd_b, dt_bias, a_log, d_skip,
                 ssd_norm_w, conv_conf_w, conv_conf_b, conf_ln_g, conf_ln_b, w_out):
    bsz, seq, _ = h.shape
    proj = h @ w_in
    a_b, a_c, a_x, s_z, s_xbc, s_dt, c_glu = jnp.split(proj, _SPLITS, axis=-1)
    y_a = a_b * causal_dwconv(a_c * a_x, conv_a_w)
    xbc = jax.nn.silu(causal_dwconv(s_xbc, conv_ssd_w, conv_ssd_b))
    s_x, s_b, s_c = jnp.split(xbc, [W_SSD, W_SSD + SSD_GROUPS * SSD_STATE], axis=-1)
    dt = jax.nn.softplus(s_dt.astype(jnp.float32) + dt_bias.astype(jnp.float32))
    a = -jnp.exp(a_log.astype(jnp.float32))
    xh = s_x.reshape(bsz, seq, SSD_HEADS, SSD_HEAD_DIM)
    y_s = ssd_chunked(xh, dt, a,
                      s_b.reshape(bsz, seq, SSD_GROUPS, SSD_STATE),
                      s_c.reshape(bsz, seq, SSD_GROUPS, SSD_STATE)).astype(h.dtype)
    y_s = (y_s + d_skip[:, None] * xh).reshape(bsz, seq, W_SSD)
    y_s = gated_rmsnorm(y_s, s_z, ssd_norm_w)
    g = c_glu[..., :W_CONF] * jax.nn.sigmoid(c_glu[..., W_CONF:])
    g = causal_dwconv(g, conv_conf_w, conv_conf_b)
    y_c = jax.nn.silu(layernorm_2(g, conf_ln_g, conf_ln_b))
    return jnp.concatenate([y_a, y_s, y_c], axis=-1) @ w_out

def swiglu(h, w_gate, w_up, w_down):
    return (jax.nn.silu(h @ w_gate) * (h @ w_up)) @ w_down

def moe_swiglu(h, w_router, w_gate, w_up, w_down):
    bsz, seq, d = h.shape
    t = bsz * seq
    m = t * TOP_K
    hf = h.reshape(t, d)
    logits = (hf @ w_router).astype(jnp.float32)
    top_vals, top_idx = lax.top_k(logits, TOP_K)
    gates = jax.nn.softmax(top_vals, axis=-1)
    flat_e = top_idx.reshape(m)
    order = jnp.argsort(flat_e)
    sorted_e = flat_e[order]
    tok = order // TOP_K
    sizes = jnp.bincount(flat_e, length=N_EXPERTS).astype(jnp.int32)
    padded = ((sizes + MOE_BLOCK - 1) // MOE_BLOCK) * MOE_BLOCK
    ends = jnp.cumsum(padded)
    starts_pad = ends - padded
    starts_sorted = jnp.cumsum(sizes) - sizes
    dest = starts_pad[sorted_e] + (jnp.arange(m, dtype=jnp.int32) - starts_sorted[sorted_e])
    cap = m + N_EXPERTS * MOE_BLOCK
    n_blocks = cap // MOE_BLOCK
    buf = jnp.zeros((cap, d), hf.dtype).at[dest].set(hf[tok])
    blk_e = jnp.minimum(jnp.searchsorted(ends, jnp.arange(n_blocks, dtype=jnp.int32) * MOE_BLOCK,
                                         side='right'), N_EXPERTS - 1)

    def expert_block(args):
        xb, e = args
        return (jax.nn.silu(xb @ w_gate[e]) * (xb @ w_up[e])) @ w_down[e]

    ybuf = lax.map(expert_block, (buf.reshape(n_blocks, MOE_BLOCK, d), blk_e)).reshape(cap, d)
    y = ybuf[dest] * gates.reshape(m)[order][:, None].astype(ybuf.dtype)
    out = jnp.zeros_like(hf).at[tok].add(y)
    return out.reshape(bsz, seq, d)

def second_inputs(seed: int = 0) -> dict:
    key = jax.random.key(seed)
    ks = jax.random.split(key, 32)
    f32 = jnp.float32

    def nrm(k, shape, scale):
        return jax.random.normal(k, shape, f32) * scale

    def gain(k, shape):
        return 1.0 + 0.02 * jax.random.normal(k, shape, f32)

    dt0 = jnp.exp(jax.random.uniform(ks[5], (DEPTH_2, SSD_HEADS), f32,
                                     math.log(1e-3), math.log(1e-1)))
    dt_bias = dt0 + jnp.log(-jnp.expm1(-dt0))
    a_log = jnp.log(jax.random.uniform(ks[6], (DEPTH_2, SSD_HEADS), f32, 1.0, 16.0))
    return {
        'x': jax.random.normal(ks[0], (BATCH, SEQ, D_MODEL), f32),
        'norm_mix': gain(ks[1], (DEPTH_2, D_MODEL)),
        'w_in': nrm(ks[2], (DEPTH_2, D_MODEL, IN_COLS), D_MODEL ** -0.5),
        'conv_a_w': nrm(ks[3], (DEPTH_2, A_CONV, W_A), A_CONV ** -0.5),
        'conv_ssd_w': nrm(ks[4], (DEPTH_2, SSD_CONV, SSD_XBC), SSD_CONV ** -0.5),
        'conv_ssd_b': nrm(ks[7], (DEPTH_2, SSD_XBC), 0.02),
        'dt_bias': dt_bias,
        'a_log': a_log,
        'd_skip': 1.0 + 0.1 * jax.random.normal(ks[8], (DEPTH_2, SSD_HEADS), f32),
        'ssd_norm_w': gain(ks[9], (DEPTH_2, W_SSD)),
        'conv_conf_w': nrm(ks[10], (DEPTH_2, CONF_KERNEL, W_CONF), CONF_KERNEL ** -0.5),
        'conv_conf_b': nrm(ks[11], (DEPTH_2, W_CONF), 0.02),
        'conf_ln_g': gain(ks[12], (DEPTH_2, W_CONF)),
        'conf_ln_b': nrm(ks[13], (DEPTH_2, W_CONF), 0.02),
        'w_out': nrm(ks[14], (DEPTH_2, D_MIX, D_MODEL), D_MIX ** -0.5),
        'norm_ffn': gain(ks[15], (DEPTH_2, D_MODEL)),
        'ffn_w_gate': nrm(ks[16], (N_DENSE, D_MODEL, D_FF), D_MODEL ** -0.5),
        'ffn_w_up': nrm(ks[17], (N_DENSE, D_MODEL, D_FF), D_MODEL ** -0.5),
        'ffn_w_down': nrm(ks[18], (N_DENSE, D_FF, D_MODEL), D_FF ** -0.5),
        'moe_router': nrm(ks[19], (N_MOE, D_MODEL, N_EXPERTS), D_MODEL ** -0.5),
        'moe_w_gate': nrm(ks[20], (N_MOE, N_EXPERTS, D_MODEL, D_FF_EXPERT), D_MODEL ** -0.5),
        'moe_w_up': nrm(ks[21], (N_MOE, N_EXPERTS, D_MODEL, D_FF_EXPERT), D_MODEL ** -0.5),
        'moe_w_down': nrm(ks[22], (N_MOE, N_EXPERTS, D_FF_EXPERT, D_MODEL), D_FF_EXPERT ** -0.5),
        'norm_final': gain(ks[23], (D_MODEL,)),
    }

def second_block(x, norm_mix, w_in, conv_a_w, conv_ssd_w, conv_ssd_b, dt_bias, a_log, d_skip,
              ssd_norm_w, conv_conf_w, conv_conf_b, conf_ln_g, conf_ln_b, w_out, norm_ffn,
              ffn_w_gate, ffn_w_up, ffn_w_down, moe_router, moe_w_gate, moe_w_up, moe_w_down,
              norm_final):
    for i in range(DEPTH_2):
        h = rmsnorm_2(x, norm_mix[i])
        x = x + hybrid_mixer(h, w_in[i], conv_a_w[i], conv_ssd_w[i], conv_ssd_b[i], dt_bias[i],
                             a_log[i], d_skip[i], ssd_norm_w[i], conv_conf_w[i], conv_conf_b[i],
                             conf_ln_g[i], conf_ln_b[i], w_out[i])
        h = rmsnorm_2(x, norm_ffn[i])
        j = i // 2
        if i % 2 == 0:
            x = x + swiglu(h, ffn_w_gate[j], ffn_w_up[j], ffn_w_down[j])
        else:
            x = x + moe_swiglu(h, moe_router[j], moe_w_gate[j], moe_w_up[j], moe_w_down[j])
    return rmsnorm_2(x, norm_final)


def setup_inputs(seed=0):
    out = dict(first_inputs(seed))
    for name, value in second_inputs(seed + 1).items():
        if name != "x":
            out[name + "_2"] = value
    return out


def reference(
    x, c, positions, ada_w, ada_b, mix_norm_g, ffn_norm_g, gm_w_in, gm_ln_g, gm_ln_b, gm_w_s,
    gm_b_s, gm_w_out, mla_w_a, mla_q_norm_g, mla_kv_norm_g, mla_w_qb, mla_w_kvb, mla_w_o, hg_lb,
    hg_w_in, hg_norm_g, hg_w_o, ff_w_up, ff_conv_w, ff_conv_b, ff_w_down, final_g, norm_mix_2,
    w_in_2, conv_a_w_2, conv_ssd_w_2, conv_ssd_b_2, dt_bias_2, a_log_2, d_skip_2, ssd_norm_w_2,
    conv_conf_w_2, conv_conf_b_2, conf_ln_g_2, conf_ln_b_2, w_out_2, norm_ffn_2, ffn_w_gate_2,
    ffn_w_up_2, ffn_w_down_2, moe_router_2, moe_w_gate_2, moe_w_up_2, moe_w_down_2,
    norm_final_2,
):
    x = first_block(
        x, c, positions, ada_w, ada_b, mix_norm_g, ffn_norm_g, gm_w_in, gm_ln_g, gm_ln_b,
        gm_w_s, gm_b_s, gm_w_out, mla_w_a, mla_q_norm_g, mla_kv_norm_g, mla_w_qb, mla_w_kvb,
        mla_w_o, hg_lb, hg_w_in, hg_norm_g, hg_w_o, ff_w_up, ff_conv_w, ff_conv_b, ff_w_down,
        final_g,
    )
    return second_block(
        x, norm_mix_2, w_in_2, conv_a_w_2, conv_ssd_w_2, conv_ssd_b_2, dt_bias_2, a_log_2,
        d_skip_2, ssd_norm_w_2, conv_conf_w_2, conv_conf_b_2, conf_ln_g_2, conf_ln_b_2, w_out_2,
        norm_ffn_2, ffn_w_gate_2, ffn_w_up_2, ffn_w_down_2, moe_router_2, moe_w_gate_2,
        moe_w_up_2, moe_w_down_2, norm_final_2,
    )


_drawn_inputs = setup_inputs


def setup_inputs(seed=0):
    import zlib

    import numpy as np

    out = dict(_drawn_inputs(seed))
    spreads = {}
    factors = {'conf_ln_g_2': 3.507,
     'conf_ln_b_2': 4.223,
     'norm_final_2': 8.125,
     'mla_q_norm_g': 3.006,
     'ssd_norm_w_2': 3.172,
     'norm_ffn_2': 2.934}
    for name, (base, spread) in spreads.items():
        noise = np.random.default_rng([zlib.crc32(name.encode()), seed]).standard_normal(out[name].shape)
        drawn = base * np.exp(spread * noise) if base else spread * noise
        out[name] = __import__('jax').numpy.asarray(drawn.astype(out[name].dtype))
    for name, factor in factors.items():
        out[name] = (out[name] * factor).astype(out[name].dtype)
    return out
```

```python
from contextlib import ExitStack

import concourse.bass as bass
from concourse import mybir
import numpy as np

F32 = mybir.dt.float32
I32 = mybir.dt.int32
ALU = mybir.AluOpType
ACT = mybir.ActivationFunctionType
AX_X = mybir.AxisListType.X

P = 128
TOK = 256
D = 1024
KD = D // P
DEPTH, DEPTH_2 = 4, 2
EPS, EPS_2 = 1e-6, 1e-5
FF = 2816
KF = FF // P
GM_INNER, GM_GROUPS = 2048, 8
KG = GM_INNER // P
HEADS = 8
Q_RANK, KV_RANK, NOPE, ROPE = 256, 128, 128, 64
ATT_SCALE = float((NOPE + ROPE) ** -0.5)
ROPE_THETA = 10000.0
W_A, W_SSD, W_CONF = 256, 512, 256
SSD_HEADS, SSD_GROUPS = 8, 2
CONF_KERNEL = 31
EXPERTS, EF = 8, 3584
KE = EF // P
LEVELS = [128, 64, 32, 16, 8, 4, 2, 1]
NEG = -1e30

RING = 4
SLAB_TILES = 16

SLABS = {
    "ada": (6 * D // 256, 16), "gm_in": (2 * GM_INNER // 256, 16), "gm_out": (8, 16),
    "mla_a": (3, 16), "mla_qb": (3, 16), "mla_kvb": (1, 16), "mla_o": (4, 16),
    "hg_in": (16, 16), "hg_o": (4, 16), "ff_up": (KF, 16), "ff_down": (16, KF // 2),
    "hy_in": (12, 16), "hy_out": (4, 16), "sw_up": (KF, 16), "sw_down": (16, KF // 2),
    "moe_up": (KE, 16), "moe_down": (16, KE // 2),
}


def program_order(stages):
    out = []
    for kind, i in stages:
        if kind == "ada":
            out += [("ada", n) for n in range(DEPTH)]
        elif kind == "gmlp":
            out += [("gm_in", i // 3), ("gm_out", i // 3)]
        elif kind == "mla":
            out += [("mla_a", 0), ("mla_qb", 0), ("mla_kvb", 0), ("mla_o", 0)]
        elif kind == "hgrn":
            out += [("hg_in", 0), ("hg_o", 0)]
        elif kind == "ffn":
            out += [("ff_up", i), ("ff_down", i)]
        elif kind == "hybrid":
            out += [("hy_in", i), ("hy_out", i)]
        elif kind == "swiglu":
            out += [("sw_up", 0), ("sw_down", 0)]
        elif kind == "moe":
            for e in range(EXPERTS):
                out += [("moe_up", e), ("moe_down", e)]
    return out


STAGES = [("ada", 0), ("gmlp", 0), ("ffn", 0), ("mla", 1), ("ffn", 1), ("hgrn", 2), ("ffn", 2),
          ("gmlp", 3), ("ffn", 3), ("final_1", 0),
          ("hybrid", 0), ("swiglu", 0), ("hybrid", 1), ("moe", 1), ("final_2", 0)]


def column_layout():
    at, n = {}, 0
    for name, cols in [
        ("c", KD), ("ada_b", DEPTH * 48), ("mix_g", DEPTH * KD), ("ffn_g", DEPTH * KD),
        ("gm_ln_g", 2 * KG), ("gm_ln_b", 2 * KG), ("q_norm", 2), ("kv_norm", 1), ("hg_lb", DEPTH * KD),
        ("hg_norm", 1), ("ff_conv", DEPTH * KF * 8), ("final_g", KD), ("norm_mix_2", 2 * KD),
        ("conv_a", 2 * 2 * 3), ("conv_ssd", 2 * 8 * 5), ("dt_bias", 2), ("a_log", 2), ("d_skip", 2 * 4),
        ("ssd_norm", 2 * 4), ("conf_conv", 2 * 2 * 32), ("conf_ln_g", 2 * 2), ("conf_ln_b", 2 * 2),
        ("norm_ffn_2", 2 * KD), ("norm_final_2", KD), ("inv_freq", 1), ("rope_sign", 1),
        ("router", KD * EXPERTS),
    ]:
        at[name] = n
        n += cols
    return at, n


COL, NCOL = column_layout()
CONST = {"mask": 0, "ident": 8 * P, "tri": 9 * P, "neg": 10 * P, "ones": 11 * P, "sel": 13 * P,
         "prior": 21 * P}
NCONST = 21 * P + 8


class Count:

    def __init__(self, sem):
        self.sem = sem
        self.seen = {}
        self.made = 0

    def tick(self):
        self.made += 1
        return self.sem

    def own(self, eng):
        eng.wait_ge(self.sem, self.made)

    def wait(self, eng, n=1):
        self.seen[eng] = self.seen.get(eng, 0) + n
        eng.wait_ge(self.sem, self.seen[eng])

    def now(self, eng):
        return self.seen.get(eng, 0)

    def skip(self, eng, n):
        self.seen[eng] = self.seen.get(eng, 0) + n


def build(nc, ins, out, stages=STAGES):
    order = program_order(stages)
    first_slab, n = {}, 0
    for sec in order:
        first_slab[sec] = n
        n += SLABS[sec[0]][0]

    with ExitStack() as ctx:
        def sb(name, shape, dt=F32):
            return ctx.enter_context(nc.sbuf_tensor(name, shape, dt))

        def sem(name):
            return ctx.enter_context(nc.semaphore(name))

        ring = sb("ring", [P, RING, SLAB_TILES * P])
        X = sb("X", [P, KD, TOK])
        H = sb("H", [P, KD, TOK])
        T = sb("T", [P, KD, TOK])
        C = sb("C", [P, 4, 2, TOK])
        A = sb("A", [P, 32, TOK])
        B = sb("B", [P, 64, TOK])
        R = sb("R", [P, 2, TOK])
        MU = sb("MU", [P, TOK])
        posi = sb("posi", [P, TOK], I32)
        rt = sb("rt", [P, 6, 2, EXPERTS])
        vec = sb("vec", [P, NCOL])
        con = sb("con", [P, NCONST])
        mod = sb("mod", [P, DEPTH * 48])
        cact = sb("cact", [P, KD])
        acol = sb("acol", [P, KD])
        gcol = sb("gcol", [P, KD])
        eps = sb("eps", [P, 2])
        wsbs = sb("wsbs", [P, 2, 2 * GM_GROUPS * P])
        small = sb("small", [P, 64])
        lbs = sb("lbs", [P, 6, KD])
        GB = sb("GB", [P, EXPERTS, TOK])
        ps = [ctx.enter_context(nc.psum_tensor(f"ps{i}", [P, 512], F32)) for i in range(8)]

        ident = con[:, CONST["ident"]:CONST["ident"] + P]
        tri = con[:, CONST["tri"]:CONST["tri"] + P]
        negm = con[:, CONST["neg"]:CONST["neg"] + P]
        ones = con[:, CONST["ones"]:CONST["ones"] + P]
        ones_wide = con[:, CONST["ones"]:CONST["ones"] + TOK]

        def V(name, i=0, n=1):
            return vec[:, COL[name] + i:COL[name] + i + n]

        def sel(h):
            return con[:, CONST["sel"] + h * P:CONST["sel"] + (h + 1) * P]

        w_ready = [sem(f"w_ready{b}") for b in range(RING)]
        in_ready = Count(sem("in_ready"))
        out_done = sem("out_done")
        slab_done = sem("slab_done")
        pe_done = Count(sem("pe_done"))
        free_act = sem("free_act")
        free_dve = sem("free_dve")
        act_step = Count(sem("act_step"))
        dve_step = Count(sem("dve_step"))
        act_done = Count(sem("act_done"))
        act_pe = Count(sem("act_pe"))
        dve_act = Count(sem("dve_act"))
        dve_pe = Count(sem("dve_pe"))
        h_ready = Count(sem("h_ready"))
        silu_done = Count(sem("silu_done"))
        g_ready = Count(sem("g_ready"))
        act_conv = sem("act_conv")
        conv_step = sem("conv_step")
        moe_sum = sem("moe_sum")
        eps_ready = sem("eps_ready")

        CREDIT = 4
        freed = {"act": CREDIT, "dve": CREDIT}

        def norm_of(kind, i):
            if kind == "final_1":
                return 0, None, X, COL["final_g"], None, None
            if kind == "final_2":
                return 1, None, H, COL["norm_final_2"], None, None
            if kind in ("hybrid", "swiglu", "moe"):
                return 1, None, H, COL["norm_mix_2" if kind == "hybrid" else "norm_ffn_2"] + i * KD, None, None
            m = i * 48 + (24 if kind == "ffn" else 0)
            return 0, m, H, COL["ffn_g" if kind == "ffn" else "mix_g"] + i * KD, m + KD, m + 2 * KD

        def run(do):
            for kind, i in stages:
                if kind != "ada":
                    do["norm"](norm_of(kind, i))
                if not kind.startswith("final"):
                    do[kind](i)

        h_total = KD * sum(norm_of(kind, i)[2] is H for kind, i in stages if kind != "ada")
        block = ctx.enter_context(nc.Block())

        def bank_uses(name):
            n = SLABS[name][0]
            who = {"gm_in": "act", "mla_a": "act", "mla_qb": "act", "mla_kvb": "act", "hg_in": "act",
                   "hy_in": "act"}.get(name, "dve")
            banks = {"gm_out": 4, "ff_down": 4, "sw_down": 4, "moe_down": 4, "mla_qb": 12,
                     "mla_kvb": 8}.get(name, n)
            return banks, who

        before, total = {}, dict(freed)
        for sec in order:
            before[sec] = dict(total)
            banks, who = bank_uses(sec[0])
            total[who] += banks
            if sec[0] == "hg_in":
                total["act"] += 4

        @block.sync
        def _(sp):
            sp.dma_start(vec[:, :], ins["vectors"]).then_inc(in_ready.sem, 16)
            sp.dma_start(con[:, :], ins["constants"]).then_inc(in_ready.sem, 16)

            for name, use in order:
                if name.startswith("moe") and use > 0:
                    continue
                n, tiles = SLABS[name]
                g0 = first_slab[(name, use)]
                src = ins["w_" + name]
                if name == "moe_down":
                    continue
                if name == "moe_up":
                    per_e = n + SLABS["moe_down"][0]
                    nd, td = SLABS["moe_down"]
                    with sp.Fori(0, EXPERTS) as e:
                        with sp.Fori(0, n // RING) as i:
                            for b in range(RING):
                                sp.wait_ge(slab_done, e * per_e + i * RING + (g0 + b - RING + 1))
                                sp.dma_start(ring[:, (g0 + b) % RING, 0:tiles * P],
                                             src[e * n + i * RING + b]).then_inc(w_ready[(g0 + b) % RING], 16)
                        with sp.Fori(0, nd // RING) as i:
                            for b in range(RING):
                                sp.wait_ge(slab_done, e * per_e + i * RING + (g0 + n + b - RING + 1))
                                sp.dma_start(ring[:, (g0 + n + b) % RING, 0:td * P],
                                             ins["w_moe_down"][e * nd + i * RING + b])\
                                  .then_inc(w_ready[(g0 + n + b) % RING], 16)
                    continue
                s = 0
                if g0 == 0:
                    for b in range(RING):
                        sp.dma_start(ring[:, b, 0:tiles * P], src[use * n + b]).then_inc(w_ready[b], 16)
                    sp.dma_start(X[:, :, :], ins["x"]).then_inc(in_ready.sem, 16)
                    sp.dma_start(wsbs[:, :, :], ins["spatial"]).then_inc(in_ready.sem, 16)
                    sp.dma_start(posi[:, :], ins["positions"]).then_inc(in_ready.sem, 16)
                    s = RING
                rounds = (n - s) // RING
                if rounds > 1:
                    with sp.Fori(0, rounds) as i:
                        for b in range(RING):
                            g = g0 + s + b
                            sp.wait_ge(slab_done, i * RING + (g - RING + 1))
                            sp.dma_start(ring[:, g % RING, 0:tiles * P],
                                         src[i * RING + (use * n + s + b)]).then_inc(w_ready[g % RING], 16)
                    s += rounds * RING
                for t in range(s, n):
                    g = g0 + t
                    sp.wait_ge(slab_done, g - RING + 1)
                    sp.dma_start(ring[:, g % RING, 0:tiles * P], src[use * n + t])\
                      .then_inc(w_ready[g % RING], 16)
            h_ready.wait(sp, h_total)
            sp.dma_start(out, H[:, :, :]).then_inc(out_done, 16)
            sp.wait_ge(out_done, 16)

        @block.tensor
        def _(pe):
            mm = nc.tensor.matmul

            def slab_wait(g, r=0):
                pe.wait_ge(w_ready[g % RING], r * 16 + 16 * (g // RING + 1))

            def banks_back(sec):
                pe.wait_ge(free_act, before[sec]["act"])
                pe.wait_ge(free_dve, before[sec]["dve"])

            def bank_wait(sec, m, r=0):
                _, who = bank_uses(sec[0])
                pe.wait_ge({"act": free_act, "dve": free_dve}[who], r + (before[sec][who] + m - 3))

            def pair(bank, slot, src, n=TOK):
                for j in range(2):
                    for k in range(KD):
                        last = mm(bank[:, j * n:(j + 1) * n], ring[:, slot, k * 256 + j * P:k * 256 + j * P + P],
                                  src[:, k, :], start=(k == 0), stop=(k == KD - 1))
                return last

            def gemm(sec, src, n=TOK, slabs=None):
                g0 = first_slab[sec]
                count = slabs or SLABS[sec[0]][0]
                banks_back(sec)
                rounds = count // 4
                s = 0
                if rounds > 1:
                    with pe.Fori(0, rounds) as i:
                        for b in range(4):
                            slab_wait(g0 + b, i)
                            bank_wait(sec, b, i * 4)
                            pair(ps[b], (g0 + b) % RING, src, n).then_inc(slab_done, 1)
                    s = rounds * 4
                for t in range(s, count):
                    slab_wait(g0 + t)
                    bank_wait(sec, t)
                    pair(ps[t % 4], (g0 + t) % RING, src, n).then_inc(slab_done, 1)

            def deep_body(sec, src, i, kt, per_tile, r0):
                g0 = first_slab[sec]
                per_slab = kt // per_tile
                s = 0
                for m in range(2):
                    pe.wait_ge(free_dve, i * 2 + r0[0] + (before[sec]["dve"] + m - 1))
                    for j in range(2):
                        for part in range(per_tile):
                            g = g0 + s
                            pe.wait_ge(w_ready[g % RING], i * (16 * per_tile) + r0[1] + 16 * (g // RING + 1))
                            for k in range(per_slab):
                                kk = part * per_slab + k
                                last = mm(ps[m][:, j * TOK:(j + 1) * TOK],
                                          ring[:, g % RING, k * P:(k + 1) * P], src[:, kk, :],
                                          start=(kk == 0), stop=(kk == kt - 1))
                            last.then_inc(slab_done, 1)
                            s += 1

            def gemm_deep(sec, src, kt, per_tile):
                banks_back(sec)
                with pe.Fori(0, 2) as i:
                    deep_body(sec, src, i, kt, per_tile, (0, 0))

            def stat(dst, tiles):
                for k, t in enumerate(tiles):
                    last = mm(dst, ones, t, start=(k == 0), stop=(k == len(tiles) - 1))
                return last

            def norm(_):
                dve_pe.wait(pe)
                stat(ps[4][:, 0:TOK], [T[:, k, :] for k in range(KD)]).then_inc(pe_done.sem, 1)

            def ada(_):
                act_pe.wait(pe)
                sec = ("ada", 0)
                g0 = first_slab[sec]
                with pe.Fori(0, DEPTH * SLABS["ada"][0] // 4) as i:
                    for b in range(4):
                        slab_wait(g0 + b, i)
                        bank_wait(sec, b, i * 4)
                        pair(ps[b], (g0 + b) % RING, cact[:, :].rearrange("p (k o) -> p k o", o=1), 1)\
                            .then_inc(slab_done, 1)

            def gmlp(i):
                j = i // 3
                h_ready.wait(pe, KD)
                gemm(("gm_in", j), H)
                pe.wait_ge(free_act, before[("gm_out", j)]["act"])
                stat(ps[4][:, 0:TOK], [A[:, KG + k, :] for k in range(KG)]).then_inc(pe_done.sem, 1)
                dve_pe.wait(pe)
                stat(ps[4][:, 256:512], [B[:, k, :] for k in range(KG)]).then_inc(pe_done.sem, 1)
                for q in range(KG // 2):
                    act_pe.wait(pe)
                    if q >= 2:
                        act_pe.wait(pe)
                    for k in range(2):
                        for c in range(2):
                            last = nc.tensor.transpose(ps[4 + q % 2][:, (2 * k + c) * P:(2 * k + c + 1) * P],
                                                       A[:, KG + 2 * q + k, c * P:(c + 1) * P], ident)
                    last.then_inc(pe_done.sem, 1)
                act_pe.wait(pe, 2)
                for q in range(KG // 2):
                    if q >= 2:
                        dve_pe.wait(pe)
                    for k in range(2):
                        for c in range(2):
                            last = mm(ps[6 + q % 2][:, (2 * k + c) * P:(2 * k + c + 1) * P],
                                      B[:, 16 + 2 * q + k, c * P:(c + 1) * P],
                                      wsbs[:, j, q * P:(q + 1) * P], start=True, stop=True)
                    last.then_inc(pe_done.sem, 1)
                dve_pe.wait(pe, 2)
                gemm_deep(("gm_out", j), A, KG, 1)

            def ffn(i):
                h_ready.wait(pe, KD)
                gemm(("ff_up", i), H)
                g_ready.wait(pe, KF)
                gemm_deep(("ff_down", i), A, KF, 2)

            def swiglu(_):
                h_ready.wait(pe, KD)
                gemm(("sw_up", 0), H)
                pe.wait_ge(free_dve, before[("sw_down", 0)]["dve"])
                gemm_deep(("sw_down", 0), A, KF, 2)

            def mla(i):
                h_ready.wait(pe, KD)
                gemm(("mla_a", 0), H)
                dve_pe.wait(pe)
                stat(ps[4][:, 0:TOK], [B[:, 0, :], B[:, 1, :]])
                stat(ps[4][:, 256:512], [B[:, 2, :]]).then_inc(pe_done.sem, 1)
                dve_pe.wait(pe)
                sec = ("mla_qb", 0)
                banks_back(sec)
                for s in range(3):
                    g = first_slab[sec] + s
                    slab_wait(g)
                    for b in range(4):
                        bank_wait(sec, 4 * s + b)
                        for j in range(2):
                            for k in range(2):
                                o = (4 * b + 2 * k + j) * P
                                last = mm(ps[b][:, j * TOK:(j + 1) * TOK], ring[:, g % RING, o:o + P],
                                          A[:, k, :], start=(k == 0), stop=(k == 1))
                        last.then_inc(slab_done if b == 3 else pe_done.sem, 1)
                sec = ("mla_kvb", 0)
                g = first_slab[sec]
                slab_wait(g)
                banks_back(sec)
                for b in range(4):
                    bank_wait(sec, b)
                    for j in range(2):
                        o = (2 * b + j) * P
                        last = mm(ps[b][:, j * TOK:(j + 1) * TOK], ring[:, g % RING, o:o + P], A[:, 2, :],
                                  start=True, stop=True)
                    last.then_inc(pe_done.sem, 1)
                for b in range(4):
                    bank_wait(sec, 4 + b)
                    t, half = b // 2, b % 2
                    last = mm(ps[b][:, :], A[:, 2, t * P:(t + 1) * P],
                              ring[:, g % RING, 1024 + half * 512:1024 + half * 512 + 512], start=True, stop=True)
                    last.then_inc(slab_done if b == 3 else pe_done.sem, 1)
                pe.wait_ge(free_act, before[("mla_o", 0)]["act"])
                dve_pe.wait(pe)

                def scores(h):
                    for q, (lo, hi) in enumerate([(0, P), (P, 384)]):
                        n = hi - lo
                        mm(ps[h % 2][:, lo:hi], B[:, 8 + h, q * P:(q + 1) * P], A[:, 8 + h, 0:n],
                           start=True, stop=False)
                        last = mm(ps[h % 2][:, lo:hi], B[:, 16 + h, q * P:(q + 1) * P], A[:, 3, 0:n],
                                  start=False, stop=True)
                    last.then_inc(pe_done.sem, 1)

                scores(0)
                for h in range(HEADS):
                    if h + 1 < HEADS:
                        scores(h + 1)
                    dve_pe.wait(pe)
                    for n in range(3):
                        last = nc.tensor.transpose(ps[2 + h % 2][:, n * P:(n + 1) * P],
                                                   T[:, 2 * (h % 2):2 * (h % 2) + 2, :]
                                                   .rearrange("p a t -> p (a t)")[:, n * P:(n + 1) * P], ident)
                    last.then_inc(pe_done.sem, 1)
                    act_pe.wait(pe, 2 if h else 1)
                    pt = T[:, 4 + 2 * (h % 2):6 + 2 * (h % 2), :].rearrange("p a t -> p (a t)")
                    v = B[:, 32:40, :].rearrange("p (t a) c -> p t (a c)", t=2)
                    mm(ps[4 + h % 2][:, 0:TOK], v[:, 0, h * P:(h + 1) * P], pt[:, 0:256], start=True, stop=False)
                    mm(ps[4 + h % 2][:, P:TOK], v[:, 1, h * P:(h + 1) * P], pt[:, 256:384], start=False, stop=True)\
                        .then_inc(pe_done.sem, 1)
                act_pe.wait(pe)
                gemm(("mla_o", 0), B[:, 40:48, :])

            def hgrn(i):
                h_ready.wait(pe, KD)
                sec = ("hg_in", 0)
                gemm(sec, H, slabs=12)
                g0 = first_slab[sec] + 12
                for b in range(4):
                    slab_wait(g0 + b)
                    bank_wait(sec, 12 + b)
                    for t in range(2):
                        for k in range(KD):
                            last = mm(ps[b][:, t * TOK:(t + 1) * TOK], H[:, k, t * P:(t + 1) * P],
                                      ring[:, (g0 + b) % RING, k * 256:(k + 1) * 256],
                                      start=(k == 0), stop=(k == KD - 1))
                    last.then_inc(slab_done, 1)
                for n, L in enumerate(LEVELS + [0]):
                    if L:
                        dve_pe.wait(pe)
                    if n:
                        dve_pe.wait(pe)
                    for h in range(HEADS):
                        q, k = (B[:, 32 + h, :], B[:, 40 + h, :]) if L else (A[:, h, :], B[:, h, :])
                        if L == 128:
                            last = mm(ps[4 + h // 4][:, (h % 4) * P:(h % 4 + 1) * P], k[:, 0:P], q[:, P:TOK],
                                      start=True, stop=True)
                        else:
                            for t in range(2):
                                o = (h % 2) * TOK + t * P
                                last = mm(ps[4 + h // 2][:, o:o + P], k[:, t * P:(t + 1) * P],
                                          q[:, t * P:(t + 1) * P], start=True, stop=True)
                    last.then_inc(pe_done.sem, 1)
                dve_pe.wait(pe, 2)
                pe.wait_ge(free_act, before[("hg_in", 0)]["act"] + 16)
                iv = A[:, 24:32, :].rearrange("p (t a) c -> p t (a c)", t=2)
                att = B[:, 48:60, :].rearrange("p a c -> p (a c)").rearrange("p (h c) -> p h c", h=HEADS)
                for h in range(HEADS):
                    o = (h % 2) * TOK
                    mm(ps[h // 2][:, o:o + TOK], iv[:, 0, h * P:(h + 1) * P], att[:, h, 0:TOK],
                       start=True, stop=False)
                    last = mm(ps[h // 2][:, o + P:o + TOK], iv[:, 1, h * P:(h + 1) * P], att[:, h, TOK:384],
                              start=False, stop=True)
                    if h % 2:
                        last.then_inc(pe_done.sem, 1)
                dve_pe.wait(pe)
                for b in range(4):
                    last = mm(ps[4 + b][:, :], ones, B[:, 8 + 2 * b:10 + 2 * b, :], start=True, stop=True)
                last.then_inc(pe_done.sem, 1)
                dve_pe.wait(pe)
                gemm(("hg_o", 0), B[:, 32:40, :])

            def hybrid(i):
                h_ready.wait(pe, KD)
                gemm(("hy_in", i), H)
                dve_pe.wait(pe)
                for n in range(4):
                    last = nc.tensor.transpose(ps[4][:, n * P:(n + 1) * P],
                                               B[:, 20 + n // 2, (n % 2) * P:(n % 2 + 1) * P], ident)
                last.then_inc(pe_done.sem, 1)
                act_pe.wait(pe)
                for t in range(2):
                    for n in range(4):
                        last = nc.tensor.transpose(ps[5 + t][:, n * P:(n + 1) * P],
                                                   B[:, 12 + n, t * P:(t + 1) * P], ident)
                last.then_inc(pe_done.sem, 1)
                pe.wait_ge(free_act, before[("hy_out", i)]["act"])
                for g in range(SSD_GROUPS):
                    dst = ps[2 + g]
                    mm(dst[:, 0:TOK], B[:, 16 + g, 0:P], B[:, 18 + g, 0:TOK], start=True, stop=True)
                    last = mm(dst[:, TOK:384], B[:, 16 + g, P:TOK], B[:, 18 + g, P:TOK], start=True, stop=True)
                last.then_inc(pe_done.sem, 1)

                def spread(h):
                    mm(ps[h % 2][:, 0:TOK], sel(h), B[:, 21, :], start=True, stop=True).then_inc(pe_done.sem, 1)

                spread(0)
                dve_pe.wait(pe)
                for h in range(SSD_HEADS):
                    if h + 1 < SSD_HEADS:
                        spread(h + 1)
                    dve_pe.wait(pe)
                    m = T[:, 4 + 2 * (h % 2):6 + 2 * (h % 2), :].rearrange("p a t -> p (a t)")
                    xd = B[:, 24 + h, :]
                    y = ps[4 + h // 2]
                    mm(y[:, 0:TOK], xd[:, 0:P], m[:, 0:TOK], start=(h % 2 == 0), stop=False)
                    last = mm(y[:, P:TOK], xd[:, P:TOK], m[:, TOK:384], start=False, stop=(h % 2 == 1))
                    if h % 2:
                        last.then_inc(pe_done.sem, 1)
                dve_pe.wait(pe)
                for g in range(SSD_GROUPS):
                    last = stat(ps[0][:, g * TOK:(g + 1) * TOK], [B[:, 48 + 2 * g + k, :] for k in range(2)])
                last.then_inc(pe_done.sem, 1)
                dve_pe.wait(pe)
                stat(ps[1][:, 0:TOK], [A[:, 2 + k, :] for k in range(2)]).then_inc(pe_done.sem, 1)
                dve_pe.wait(pe)
                stat(ps[1][:, TOK:512], [A[:, 4 + k, :] for k in range(2)]).then_inc(pe_done.sem, 1)
                act_pe.wait(pe)
                dve_pe.wait(pe)
                gemm(("hy_out", i), B[:, 56:64, :])

            def moe(_):
                h_ready.wait(pe, KD)
                banks_back(("moe_up", 0))
                for t in range(2):
                    for k in range(KD):
                        last = mm(ps[4][:, t * 8:(t + 1) * 8], H[:, k, t * P:(t + 1) * P],
                                  V("router", k * EXPERTS, EXPERTS), start=(k == 0), stop=(k == KD - 1))
                last.then_inc(pe_done.sem, 1)
                dve_pe.wait(pe)
                for t in range(2):
                    last = nc.tensor.transpose(ps[5][:, t * P:(t + 1) * P], B[:, 0, t * P:(t + 1) * P], ident)
                last.then_inc(pe_done.sem, 1)
                act_pe.wait(pe)
                for e in range(EXPERTS):
                    last = mm(ps[4 + e // 2][:, (e % 2) * TOK:(e % 2 + 1) * TOK], sel(e), B[:, 1, :],
                              start=True, stop=True)
                last.then_inc(pe_done.sem, 1)
                nu, nd = SLABS["moe_up"][0], SLABS["moe_down"][0]
                up, down = ("moe_up", 0), ("moe_down", 0)
                per_e = (nu + 4)
                per_w = (nu + nd) // RING
                gu = first_slab[up]
                with pe.Fori(0, EXPERTS) as e:
                    with pe.Fori(0, nu // 4) as i:
                        pe.wait_ge(free_dve, e * per_e + before[up]["dve"])
                        for b in range(4):
                            pe.wait_ge(w_ready[(gu + b) % RING],
                                       e * (16 * per_w) + i * 16 + 16 * ((gu + b) // RING + 1))
                            pe.wait_ge(free_dve, e * per_e + i * 4 + (before[up]["dve"] + b - 3))
                            pair(ps[b], (gu + b) % RING, H).then_inc(slab_done, 1)
                    with pe.Fori(0, 2) as i:
                        pe.wait_ge(free_dve, e * per_e + before[down]["dve"])
                        deep_body(down, A, i, KE, 2, (e * per_e, e * (16 * per_w)))

            in_ready.wait(pe, 80)
            run({"norm": norm, "ada": ada, "gmlp": gmlp, "ffn": ffn, "mla": mla, "hgrn": hgrn,
                 "hybrid": hybrid, "swiglu": swiglu, "moe": moe})

        @block.scalar
        def _(act):
            af = nc.scalar.activation

            def step(ins):
                ins.then_inc(act_step.tick(), 1)
                act_step.own(act)

            def evac(sec, func, dst, count=None, m0=0):
                g0 = first_slab[sec] + m0
                count = count or SLABS[sec[0]][0]
                rounds = count // 4
                s = 0
                if rounds > 1:
                    with act.Fori(0, rounds) as i:
                        for b in range(4):
                            act.wait_ge(slab_done, i * 4 + (g0 + b + 1))
                            af(dst(i * 4 + b), ps[b][:, :], func).then_inc(free_act, 1)
                    s = rounds * 4
                for t in range(s, count):
                    act.wait_ge(slab_done, g0 + t + 1)
                    af(dst(t), ps[t % 4][:, :], func).then_inc(free_act, 1)

            def root(dst, src, n, e=0):
                return af(dst, src, ACT.Sqrt, bias=eps[:, e:e + 1], scale=1.0 / n)

            def tiles(buf, m0=0):
                return lambda m: buf[:, bass.ds(m * 2 + m0, 2), :].rearrange("p a t -> p (a t)")

            def norm(arg):
                e, shift = arg[0], arg[1]
                pe_done.wait(act)
                root(R[:, 0, :], ps[4][:, 0:TOK], D, e).then_inc(act_done.tick(), 1)
                if shift is not None:
                    for k in range(KD):
                        dve_act.wait(act)
                        af(H[:, k, :], T[:, k, :], ACT.Identity, bias=mod[:, shift + k:shift + k + 1])\
                            .then_inc(h_ready.sem, 1)

            def ada(_):
                af(cact[:, :], V("c", 0, KD), ACT.Silu).then_inc(act_pe.tick(), 1)

            def gmlp(i):
                j = i // 3
                evac(("gm_in", j), ACT.Gelu_apprx_tanh, tiles(A))
                pe_done.skip(act, 1)
                pe_done.wait(act)
                root(R[:, 0, :], ps[4][:, 256:512], GM_INNER).then_inc(act_done.tick(), 1)
                dve_act.wait(act)
                for k in range(KG):
                    ins = af(A[:, KG + k, :], A[:, KG + k, :], ACT.Identity,
                             bias=V("gm_ln_b", j * KG + k), scale=V("gm_ln_g", j * KG + k))
                    if k % 2:
                        ins.then_inc(act_pe.tick(), 1)
                        q = k // 2
                        if q >= 1:
                            copy_vt(q - 1)
                copy_vt(KG // 2 - 1)
                pe_done.skip(act, KG // 2)

            def copy_vt(q):
                pe_done.wait(act)
                af(B[:, 16 + 2 * q:18 + 2 * q, :].rearrange("p a t -> p (a t)"), ps[4 + q % 2][:, :],
                   ACT.Copy).then_inc(act_pe.tick(), 1)

            def ffn(i):
                sec = ("ff_up", i)
                g0 = first_slab[sec]
                f0 = before[sec]["dve"]

                def one(m, b, i4):
                    act.wait_ge(slab_done, i4 + (g0 + b + 1))
                    act.wait_ge(free_dve, i4 + (f0 + b))
                    for half in range(2):
                        c = m * 8 + (COL["ff_conv"] + i * KF * 8 + half * 4)
                        ins = af(C[:, b % 4, half, :], ps[b % 4][:, half * TOK:(half + 1) * TOK], ACT.Identity,
                                 bias=vec[:, bass.ds(c + 3, 1)], scale=vec[:, bass.ds(c + 2, 1)])
                    ins.then_inc(act_conv, 1)
                    act.wait_ge(free_dve, i4 + (f0 + b + 1))
                    af(C[:, b % 4, 0, :], C[:, b % 4, 0, :], ACT.Silu).then_inc(silu_done.sem, 1)

                with act.Fori(0, KF // 4) as r:
                    for b in range(4):
                        one(r * 4 + b, b, r * 4)
                for m in range(KF // 4 * 4, KF):
                    one(m, m, 0)

            def swiglu(_):
                g0 = first_slab[("sw_up", 0)]
                with act.Fori(0, KF // 4) as i:
                    for b in range(4):
                        act.wait_ge(slab_done, i * 4 + (g0 + b + 1))
                        af(C[:, b, 0, :], ps[b][:, 0:TOK], ACT.Silu).then_inc(silu_done.sem, 1)
                for m in range(KF // 4 * 4, KF):
                    act.wait_ge(slab_done, g0 + m + 1)
                    af(C[:, m % 4, 0, :], ps[m % 4][:, 0:TOK], ACT.Silu).then_inc(silu_done.sem, 1)

            def mla(_):
                dve_act.wait(act)
                af(B[:, 60, :], B[:, 60, :], ACT.Sin)
                af(B[:, 61, :], B[:, 61, :], ACT.Sin).then_inc(act_done.tick(), 1)
                evac(("mla_a", 0), ACT.Copy, tiles(A))
                pe_done.wait(act)
                root(R[:, 0, :], ps[4][:, 0:TOK], Q_RANK)
                root(R[:, 1, :], ps[4][:, 256:512], KV_RANK).then_inc(act_done.tick(), 1)
                g = first_slab[("mla_qb", 0)]
                for m in range(12):
                    if m % 4 == 3:
                        act.wait_ge(slab_done, g + m // 4 + 1)
                    else:
                        pe_done.wait(act)
                    af(B[:, 8 + 2 * m:10 + 2 * m, :].rearrange("p a t -> p (a t)"), ps[m % 4][:, :], ACT.Copy)\
                        .then_inc(free_act, 1)
                g = first_slab[("mla_kvb", 0)]
                for b in range(4):
                    pe_done.wait(act)
                    af(A[:, 8 + 2 * b:10 + 2 * b, :].rearrange("p a t -> p (a t)"), ps[b][:, :], ACT.Copy)\
                        .then_inc(free_act, 1)
                for b in range(4):
                    if b == 3:
                        act.wait_ge(slab_done, g + 1)
                    else:
                        pe_done.wait(act)
                    af(B[:, 32 + 2 * b:34 + 2 * b, :].rearrange("p a t -> p (a t)"), ps[b][:, :], ACT.Copy)\
                        .then_inc(free_act, 1)
                for h in range(HEADS):
                    s = T[:, 2 * (h % 2):2 * (h % 2) + 2, :].rearrange("p a t -> p (a t)")
                    dve_act.wait(act)
                    o = 8 * (h % 2)
                    af(s[:, 0:P], s[:, 0:P], ACT.Exp, bias=small[:, o + 2:o + 3], accum_out=small[:, o + 4:o + 5])
                    af(s[:, P:384], s[:, P:384], ACT.Exp, bias=small[:, o + 3:o + 4],
                       accum_out=small[:, o + 5:o + 6]).then_inc(act_done.tick(), 1)
                    if h + 1 < HEADS:
                        pe_done.skip(act, 1)
                    if h == 0:
                        pe_done.skip(act, 1)
                    pe_done.wait(act)
                    af(T[:, 4 + 2 * (h % 2):6 + 2 * (h % 2), :].rearrange("p a t -> p (a t)")[:, 0:384],
                       ps[2 + h % 2][:, 0:384], ACT.Copy).then_inc(act_pe.tick(), 1)
                    pe_done.wait(act)
                    af(B[:, 40 + h, :], ps[4 + h % 2][:, 0:TOK], ACT.Copy).then_inc(act_pe.tick(), 1)

            def hgrn(_):
                dve_act.wait(act)
                af(lbs[:, 0:4, :], lbs[:, 0:4, :], ACT.Exp).then_inc(act_done.tick(), 1)
                evac(("hg_in", 0), ACT.Copy, tiles(A), count=12)
                act.wait_ge(free_act, before[("hg_in", 0)]["act"] + 12)
                af(A[:, 8:16, :], A[:, 8:16, :], ACT.Sigmoid).then_inc(act_done.tick(), 1)
                g0 = first_slab[("hg_in", 0)] + 12
                iv = A[:, 24:32, :].rearrange("p (t a) c -> p t (a c)", t=2)
                for b in range(4):
                    act.wait_ge(slab_done, g0 + b + 1)
                    af(iv[:, :, b * TOK:(b + 1) * TOK], ps[b][:, :].rearrange("p (t c) -> p t c", t=2), ACT.Copy)\
                        .then_inc(free_act, 1)
                dve_act.wait(act)
                af(B[:, 8:16, :], B[:, 8:16, :], ACT.Ln).then_inc(act_done.tick(), 1)
                for _ in LEVELS:
                    dve_act.wait(act)
                    step(af(B[:, 24:32, :], B[:, 24:32, :], ACT.Abs))
                    af(B[:, 24:32, :], B[:, 24:32, :], ACT.Exp, scale=-1.0).then_inc(act_done.tick(), 1)
                pe_done.skip(act, len(LEVELS) + 1)
                for b in range(4):
                    pe_done.wait(act)
                    af(B[:, 2 * b:2 * b + 2, :].rearrange("p a t -> p (a t)"), ps[b][:, :], ACT.Copy)\
                        .then_inc(free_act, 1)
                af(B[:, 24:32, :], A[:, 16:24, :], ACT.Silu)
                pe_done.wait(act)
                for b in range(4):
                    ins = root(B[:, 16 + 2 * b:18 + 2 * b, :].rearrange("p a t -> p (a t)"), ps[4 + b][:, :], P)
                ins.then_inc(act_done.tick(), 1)

            def hybrid(i):
                evac(("hy_in", i), ACT.Copy, tiles(A))
                dve_act.wait(act)
                step(af(B[:, 20, :], B[:, 20, :], ACT.Exp))
                af(B[:, 20, :], B[:, 20, :], ACT.Ln, bias=ones[:, 0:1])
                af(small[:, 0:1], V("a_log", i), ACT.Exp).then_inc(act_done.tick(), 1)
                pe_done.wait(act)
                af(B[:, 22:24, :].rearrange("p a t -> p (a t)"), ps[4][:, :], ACT.Copy).then_inc(act_done.tick(), 1)
                dve_act.wait(act)
                af(B[:, 12:20, :], B[:, 4:12, :], ACT.Silu).then_inc(act_pe.tick(), 1)
                af(B[:, 40:44, :], A[:, 6:10, :], ACT.Silu)
                af(A[:, 20:22, :], A[:, 20:22, :], ACT.Sigmoid).then_inc(act_done.tick(), 1)
                pe_done.skip(act, 2)
                for h in range(SSD_HEADS):
                    dve_act.wait(act)
                    m = T[:, 4 + 2 * (h % 2):6 + 2 * (h % 2), :].rearrange("p a t -> p (a t)")[:, 0:384]
                    af(m, m, ACT.Exp).then_inc(act_done.tick(), 1)
                pe_done.skip(act, SSD_HEADS + SSD_HEADS // 2)
                pe_done.wait(act)
                root(B[:, 52:54, :].rearrange("p a t -> p (a t)"), ps[0][:, :], 256, 1).then_inc(act_done.tick(), 1)
                pe_done.skip(act, 1)
                pe_done.wait(act)
                root(R[:, 0, :], ps[1][:, TOK:512], W_CONF, 1).then_inc(act_done.tick(), 1)
                dve_act.wait(act)
                for k in range(2):
                    ins = af(B[:, 62 + k, :], A[:, 2 + k, :], ACT.Silu, bias=V("conf_ln_b", i * 2 + k),
                             scale=V("conf_ln_g", i * 2 + k))
                ins.then_inc(act_pe.tick(), 1)

            def moe(_):
                pe_done.skip(act, 1)
                dve_act.wait(act)
                af(small[:, 40:42], small[:, 38:40], ACT.Exp).then_inc(act_done.tick(), 1)
                pe_done.wait(act)
                af(B[:, 1, :], ps[5][:, 0:TOK], ACT.Copy).then_inc(act_pe.tick(), 1)
                pe_done.wait(act)
                for b in range(4):
                    ins = af(GB[:, 2 * b:2 * b + 2, :].rearrange("p a t -> p (a t)"), ps[4 + b][:, :], ACT.Copy)
                ins.then_inc(act_done.tick(), 1)
                nu, nd = SLABS["moe_up"][0], SLABS["moe_down"][0]
                g0 = first_slab[("moe_up", 0)]
                with act.Fori(0, EXPERTS) as e:
                    with act.Fori(0, nu // 4) as i:
                        for b in range(4):
                            act.wait_ge(slab_done, e * (nu + nd) + i * 4 + (g0 + b + 1))
                            af(C[:, b, 0, :], ps[b][:, 0:TOK], ACT.Silu).then_inc(silu_done.sem, 1)

            in_ready.wait(act, 80)
            act.wait_ge(eps_ready, 2)
            run({"norm": norm, "ada": ada, "gmlp": gmlp, "ffn": ffn, "mla": mla, "hgrn": hgrn,
                 "hybrid": hybrid, "swiglu": swiglu, "moe": moe})

        @block.vector
        def _(dve):
            tt, ts, stt = nc.vector.tensor_tensor, nc.vector.tensor_scalar, nc.vector.scalar_tensor_tensor

            def step(ins):
                ins.then_inc(dve_step.tick(), 1)
                dve_step.own(dve)

            def wide(ap, n):
                return ap.rearrange("p (o t) -> p o t", o=1).to_broadcast([P, n, TOK])

            def residual(sec, per_bank, gated):
                g0 = first_slab[sec]
                for m in range(4):
                    dve.wait_ge(slab_done, g0 + per_bank * (m + 1))
                    b = m % 4 if per_bank == 1 else m % 2
                    if gated:
                        for j in range(2):
                            k = 2 * m + j
                            ins = stt(out=X[:, k, :], in0=ps[b][:, j * TOK:(j + 1) * TOK],
                                      scalar=gcol[:, k:k + 1], in1=X[:, k, :], op0=ALU.mult, op1=ALU.add)
                    else:
                        xs = X[:, 2 * m:2 * m + 2, :].rearrange("p a t -> p (a t)")
                        ins = tt(xs, xs, ps[b][:, :], ALU.add)
                    ins.then_inc(free_dve, 1)
                dve.wait_ge(free_dve, before[sec]["dve"] + 4)

            def norm(arg):
                _, shift, dst, gain, scale, gate = arg
                pe_done.skip(dve, 1)
                tt(T[:, :, :], X[:, :, :], X[:, :, :], ALU.mult).then_inc(dve_pe.tick(), 1)
                if shift is not None:
                    stt(out=acol[:, :], in0=mod[:, scale:scale + KD], scalar=1.0, in1=vec[:, gain:gain + KD],
                        op0=ALU.add, op1=ALU.mult)
                    step(ts(gcol[:, :], mod[:, gate:gate + KD], 1.0, None, ALU.add))
                act_done.wait(dve)
                step(nc.vector.reciprocal(R[:, 0, :], R[:, 0, :]))
                for k in range(KD):
                    col = acol[:, k:k + 1] if shift is not None else vec[:, gain + k:gain + k + 1]
                    to = T if shift is not None else dst
                    ins = stt(out=to[:, k, :], in0=X[:, k, :], scalar=col, in1=R[:, 0, :],
                              op0=ALU.mult, op1=ALU.mult)
                    if shift is not None:
                        ins.then_inc(dve_act.tick(), 1)
                    elif dst is X:
                        if k == KD - 1:
                            step(ins)
                    else:
                        ins.then_inc(h_ready.sem, 1)

            def ada(_):
                with dve.Fori(0, DEPTH * SLABS["ada"][0] // 4) as i:
                    for b in range(4):
                        dve.wait_ge(slab_done, i * 4 + (b + 1))
                        tt(mod[:, bass.ds(i * 8 + 2 * b, 2)], ps[b][:, 0:2],
                           vec[:, bass.ds(i * 8 + (COL["ada_b"] + 2 * b), 2)], ALU.add).then_inc(free_dve, 1)
                dve.wait_ge(free_dve, CREDIT + DEPTH * SLABS["ada"][0])

            def gmlp(i):
                j = i // 3
                v = A[:, KG:2 * KG, :]
                ws = wsbs[:, j, 0:GM_GROUPS * P].rearrange("p (g t) -> p g t", g=GM_GROUPS)
                tt(ws, ws, tri.rearrange("p (o t) -> p o t", o=1).to_broadcast([P, GM_GROUPS, P]), ALU.mult)
                pe_done.wait(dve)
                step(ts(MU[:, :], ps[4][:, 0:TOK], 1.0 / GM_INNER, None, ALU.mult))
                step(tt(v, v, wide(MU[:, :], KG), ALU.subtract))
                tt(B[:, 0:KG, :], v, v, ALU.mult).then_inc(dve_pe.tick(), 1)
                pe_done.skip(dve, 1)
                act_done.wait(dve)
                step(nc.vector.reciprocal(R[:, 0, :], R[:, 0, :]))
                tt(v, v, wide(R[:, 0, :], KG), ALU.mult).then_inc(dve_act.tick(), 1)
                pe_done.skip(dve, KG // 2)
                for q in range(KG // 2):
                    pe_done.wait(dve)
                    t = T[:, 2 * (q % 2):2 * (q % 2) + 2, :].rearrange("p a t -> p (a t)")
                    bs = wsbs[:, j, (GM_GROUPS + q) * P:(GM_GROUPS + q + 1) * P]
                    step(tt(t.rearrange("p (r c) -> p r c", c=P), ps[6 + q % 2][:, :].rearrange("p (r c) -> p r c", c=P),
                            bs.rearrange("p (o c) -> p o c", o=1).to_broadcast([P, 4, P]), ALU.add))
                    u = A[:, 2 * q:2 * q + 2, :].rearrange("p a t -> p (a t)")
                    tt(u, u, t, ALU.mult).then_inc(dve_pe.tick(), 1)
                residual(("gm_out", j), 2, True)

            def ffn(i):
                sec = ("ff_up", i)

                def one(m, b, i4):
                    dve.wait_ge(act_conv, i4 + (i * KF + b + 1))
                    for d in (1, 2):
                        for half in range(2):
                            c = m * 8 + (COL["ff_conv"] + i * KF * 8 + half * 4)
                            o = C[:, b % 4, half, d:TOK]
                            ins = stt(out=o, in0=ps[b % 4][:, half * TOK:(half + 1) * TOK - d],
                                      scalar=vec[:, bass.ds(c + (2 - d), 1)], in1=o, op0=ALU.mult, op1=ALU.add)
                        if d == 1:
                            ins.then_inc(conv_step, 1)
                            dve.wait_ge(conv_step, i4 + (i * KF + b + 1))
                    ins.then_inc(free_dve, 1)
                    dve.wait_ge(free_dve, i4 + (before[sec]["dve"] + b + 1))
                    dve.wait_ge(silu_done.sem, i4 + (silu_done.now(dve) + b + 1))
                    tt(A[:, bass.ds(m * 1, 1), :], C[:, b % 4, 0:1, :], C[:, b % 4, 1:2, :], ALU.mult)\
                        .then_inc(g_ready.sem, 1)

                with dve.Fori(0, KF // 4) as r:
                    for b in range(4):
                        one(r * 4 + b, b, r * 4)
                for m in range(KF // 4 * 4, KF):
                    one(m, m, 0)
                silu_done.skip(dve, KF)
                residual(("ff_down", i), 4, True)

            def swiglu(_):
                s0 = silu_done.now(dve)
                with dve.Fori(0, KF // 4) as i:
                    for b in range(4):
                        dve.wait_ge(silu_done.sem, i * 4 + (s0 + b + 1))
                        tt(A[:, bass.ds(i * 4 + b, 1), :].rearrange("p a t -> p (a t)"), C[:, b, 0, :],
                           ps[b][:, TOK:512], ALU.mult).then_inc(free_dve, 1)
                for m in range(KF // 4 * 4, KF):
                    dve.wait_ge(silu_done.sem, s0 + m + 1)
                    tt(A[:, m, :], C[:, m % 4, 0, :], ps[m % 4][:, TOK:512], ALU.mult).then_inc(free_dve, 1)
                silu_done.skip(dve, KF)
                residual(("sw_down", 0), 4, False)

            def mla(_):
                ang, k, s, c = B[:, 62, :], B[:, 63, :], B[:, 60, :], B[:, 61, :]
                step(nc.vector.tensor_copy(B[:, 59, :], posi[:, :]))
                step(ts(ang, B[:, 59, :], V("inv_freq"), None, ALU.mult))
                step(ts(k, ang, float(1 / (2 * np.pi)), 12582912.0, ALU.mult, ALU.add))
                step(ts(k, k, 12582912.0, None, ALU.subtract))
                for part in (6.28125, float(np.float32(0.0019350051879882812)), float(2 * np.pi - 6.28125 - 0.0019350051879882812)):
                    step(stt(out=ang, in0=k, scalar=-part, in1=ang, op0=ALU.mult, op1=ALU.add))
                step(ts(ang, ang, float(np.float32(3.1415925)), -float(np.float32(3.1415925)), ALU.min, ALU.max))
                step(ts(k, ang, -1.0, None, ALU.mult))
                step(tt(k, k, ang, ALU.min))
                ts(c, k, float(np.pi / 2), None, ALU.add)
                ts(s, ang, V("rope_sign"), None, ALU.mult).then_inc(dve_act.tick(), 1)
                act_done.wait(dve)
                dve.wait_ge(free_act, before[("mla_a", 0)]["act"] + 3)
                tt(B[:, 0:3, :], A[:, 0:3, :], A[:, 0:3, :], ALU.mult).then_inc(dve_pe.tick(), 1)
                tt(B[:, 3, :], A[:, 3, :], c, ALU.mult)
                step(tt(B[:, 4, :], A[:, 4, :], s, ALU.mult))
                step(tt(A[:, 3, :], B[:, 3, :], B[:, 4, :], ALU.add))
                act_done.wait(dve)
                step(nc.vector.reciprocal(R[:, :, :], R[:, :, :]))
                for t in range(3):
                    g = V("q_norm", t) if t < 2 else V("kv_norm")
                    ins = stt(out=A[:, t, :], in0=A[:, t, :], scalar=g, in1=R[:, t // 2, :],
                              op0=ALU.mult, op1=ALU.mult)
                ins.then_inc(dve_pe.tick(), 1)
                dve.wait_ge(free_act, before[("mla_qb", 0)]["act"] + 12)
                tt(B[:, 16:24, :], B[:, 16:24, :], wide(c, 8), ALU.mult)
                step(tt(B[:, 24:32, :], B[:, 24:32, :], wide(s, 8), ALU.mult))
                tt(B[:, 16:24, :], B[:, 16:24, :], B[:, 24:32, :], ALU.add).then_inc(dve_pe.tick(), 1)
                pe_done.skip(dve, 1 + 9 + 7)
                for h in range(HEADS):
                    if h < 1:
                        pe_done.wait(dve)
                    o = 8 * (h % 2)
                    s_ = T[:, 2 * (h % 2):2 * (h % 2) + 2, :].rearrange("p a t -> p (a t)")
                    b = ps[h % 2]
                    for lo in (0, TOK):
                        stt(out=s_[:, lo:lo + P], in0=b[:, lo:lo + P], scalar=ATT_SCALE, in1=negm,
                            op0=ALU.mult, op1=ALU.add)
                    step(ts(s_[:, P:TOK], b[:, P:TOK], ATT_SCALE, None, ALU.mult))
                    nc.vector.tensor_reduce(small[:, o:o + 1], s_[:, 0:P], AX_X, ALU.max)
                    step(nc.vector.tensor_reduce(small[:, o + 1:o + 2], s_[:, P:384], AX_X, ALU.max))
                    ts(small[:, o + 2:o + 4], small[:, o:o + 2], -1.0, None, ALU.mult).then_inc(dve_act.tick(), 1)
                    act_done.wait(dve)
                    step(nc.vector.reciprocal(small[:, o + 6:o + 8], small[:, o + 4:o + 6]))
                    ts(s_[:, 0:P], s_[:, 0:P], small[:, o + 6:o + 7], None, ALU.mult)
                    ts(s_[:, P:384], s_[:, P:384], small[:, o + 7:o + 8], None, ALU.mult).then_inc(dve_pe.tick(), 1)
                    if h + 1 < HEADS:
                        pe_done.wait(dve)
                    pe_done.skip(dve, 2)
                residual(("mla_o", 0), 1, True)

            def hgrn(_):
                lb = lbs[:, 0:4, :]
                src = vec[:, COL["hg_lb"]:COL["hg_lb"] + DEPTH * KD].rearrange("p (d k) -> p d k", d=DEPTH)
                step(tt(lbs[:, 4:6, :], src[:, 0:2, :], src[:, 2:4, :], ALU.max))
                step(tt(lbs[:, 4, :], lbs[:, 4, :], lbs[:, 5, :], ALU.max))
                tt(lb, src, lbs[:, 4:5, :].to_broadcast([P, 4, KD]), ALU.subtract).then_inc(dve_act.tick(), 1)
                act_done.wait(dve)
                step(tt(lbs[:, 4:6, :], lbs[:, 0:2, :], lbs[:, 2:4, :], ALU.add))
                step(tt(lbs[:, 4, :], lbs[:, 4, :], lbs[:, 5, :], ALU.add))
                step(nc.vector.reciprocal(lbs[:, 4, :], lbs[:, 4, :]))
                step(tt(lbs[:, 5, :], lbs[:, 1, :], lbs[:, 2, :], ALU.add))
                step(tt(lbs[:, 0, :], lbs[:, 5, :], lbs[:, 4, :], ALU.mult))
                step(ts(lbs[:, 1, :], lbs[:, 0, :], -1.0, 1.0, ALU.mult, ALU.add))
                act_done.wait(dve)
                for k in range(KD):
                    ins = ts(B[:, 8 + k, :], A[:, 8 + k, :], lbs[:, 1, k:k + 1], lbs[:, 0, k:k + 1],
                             ALU.mult, ALU.add)
                step(ins)
                ts(B[:, 0:8, :], B[:, 8:16, :], -1.0, 1.0, ALU.mult, ALU.add).then_inc(dve_act.tick(), 1)
                act_done.wait(dve)
                for k in range(KD):
                    ins = nc.vector.tensor_tensor_scan(B[:, 16 + k, :], ones_wide, B[:, 8 + k, :], 0.0,
                                                       ALU.mult, ALU.add)
                step(ins)
                att = B[:, 48:60, :].rearrange("p a c -> p (a c)").rearrange("p (h r c) -> p h r c", h=HEADS, r=3)
                bc = B[:, 16:24, :].rearrange("p a c -> p (a c)")
                dd = B[:, 24:32, :].rearrange("p a c -> p (a c)")

                def gather(n):
                    pe_done.wait(dve)
                    if n == 0:
                        for b in range(2):
                            ins = nc.vector.tensor_copy(att[:, 4 * b:4 * b + 4, 1, :],
                                                        ps[4 + b][:, :].rearrange("p (h c) -> p h c", c=P))
                        ins.then_inc(dve_pe.tick(), 1)
                        return
                    m = con[:, CONST["mask"] + (n - 1) * P:CONST["mask"] + n * P]
                    m = m.rearrange("p (o c) -> p o c", o=1).to_broadcast([P, 4, P])
                    for b in range(4):
                        ins = tt(T[:, 2 * b:2 * b + 2, :].rearrange("p a (r c) -> p (a r) c", c=P),
                                 ps[4 + b][:, :].rearrange("p (r c) -> p r c", c=P), m, ALU.mult)
                    ins.then_inc(dve_pe.tick(), 1)
                    dve_pe.own(dve)
                    t4 = T[:, :, :].rearrange("p h (r c) -> p h r c", c=P)
                    if n == 1:
                        step(nc.vector.tensor_copy(att[:, :, 0:3:2, :], t4))
                    else:
                        ins = tt(att[:, :, 0:3:2, :], att[:, :, 0:3:2, :], t4, ALU.add)
                        if n == len(LEVELS):
                            ins.then_inc(dve_pe.tick(), 1)
                        else:
                            step(ins)

                for n, L in enumerate(LEVELS):
                    g = 8 * TOK // (2 * L)
                    bv = bc.rearrange("p (g l) -> p g l", l=2 * L)
                    if n:
                        dve_pe.own(dve)
                    tt(dd.rearrange("p (g l) -> p g l", l=2 * L), bv,
                       bv[:, :, L - 1:L].to_broadcast([P, g, 2 * L]), ALU.subtract).then_inc(dve_act.tick(), 1)
                    if n:
                        gather(n - 1)
                    act_done.wait(dve)
                    tt(B[:, 32:40, :], A[:, 0:8, :], B[:, 24:32, :], ALU.mult)
                    tt(B[:, 40:48, :], B[:, 0:8, :], B[:, 24:32, :], ALU.mult).then_inc(dve_pe.tick(), 1)
                gather(len(LEVELS) - 1)
                gather(len(LEVELS))
                dve.wait_ge(free_act, before[("hg_in", 0)]["act"] + 20)
                tt(B[:, 8:16, :], B[:, 0:8, :], B[:, 0:8, :], ALU.mult).then_inc(dve_pe.tick(), 1)
                pe_done.skip(dve, 5)
                act_done.wait(dve)
                step(nc.vector.reciprocal(B[:, 16:24, :], B[:, 16:24, :]))
                step(stt(out=B[:, 0:8, :], in0=B[:, 0:8, :], scalar=V("hg_norm"), in1=B[:, 16:24, :],
                         op0=ALU.mult, op1=ALU.mult))
                tt(B[:, 32:40, :], B[:, 0:8, :], B[:, 24:32, :], ALU.mult).then_inc(dve_pe.tick(), 1)
                residual(("hg_o", 0), 1, True)

            def causal_conv(dst, src, n, col, taps, bias):
                for k in range(n):
                    w = col(k)
                    if bias:
                        ins = ts(dst(k), src(k), vec[:, w + taps - 1:w + taps], vec[:, w + taps:w + taps + 1],
                                 ALU.mult, ALU.add)
                    else:
                        ins = ts(dst(k), src(k), vec[:, w + taps - 1:w + taps], None, ALU.mult)
                for d in range(1, taps):
                    step(ins)
                    for k in range(n):
                        c = col(k) + taps - 1 - d
                        ins = stt(out=dst(k)[:, d:TOK], in0=src(k)[:, 0:TOK - d], scalar=vec[:, c:c + 1],
                                  in1=dst(k)[:, d:TOK], op0=ALU.mult, op1=ALU.add)
                return ins

            def hybrid(i):
                dve.wait_ge(free_act, before[("hy_in", i)]["act"] + SLABS["hy_in"][0])
                step(ts(B[:, 22, :], A[:, 22, :], V("dt_bias", i), None, ALU.add))
                step(ts(B[:, 21, :], B[:, 22, :], -1.0, None, ALU.mult))
                tt(B[:, 20, :], B[:, 21, :], B[:, 22, :], ALU.min).then_inc(dve_act.tick(), 1)
                step(ts(B[:, 22, :], B[:, 22, :], 0.0, None, ALU.max))
                nc.vector.memset(B[:, 24:32, :], 0.0)
                act_done.wait(dve)
                step(tt(B[:, 20, :], B[:, 20, :], B[:, 22, :], ALU.add))
                step(ts(B[:, 23, :], B[:, 20, :], small[:, 0:1], -1.0, ALU.mult, ALU.mult))
                nc.vector.tensor_tensor_scan(B[:, 21, :], ones_wide, B[:, 23, :], 0.0, ALU.mult, ALU.add)\
                    .then_inc(dve_pe.tick(), 1)
                causal_conv(lambda k: B[:, 4 + k, :], lambda k: A[:, 10 + k, :], 8,
                            lambda k: COL["conv_ssd"] + (i * 8 + k) * 5, 4, True).then_inc(dve_act.tick(), 1)
                step(tt(B[:, 0:2, :], A[:, 2:4, :], A[:, 4:6, :], ALU.mult))
                step(causal_conv(lambda k: B[:, 2 + k, :], lambda k: B[:, k, :], 2,
                                 lambda k: COL["conv_a"] + (i * 2 + k) * 3, 3, False))
                tt(B[:, 56:58, :], A[:, 0:2, :], B[:, 2:4, :], ALU.mult)
                act_done.wait(dve)
                act_done.wait(dve)
                pe_done.wait(dve, 2)
                cols = B[:, 22:24, :].rearrange("p a (r c) -> p (a r) c", c=P)
                for h in range(SSD_HEADS):
                    for t in range(2):
                        o = t * P + (h % 2) * 64
                        ins = ts(B[:, 24 + h, o:o + 64], ps[5 + t][:, h * 64:(h + 1) * 64],
                                 cols[:, t, h:h + 1], None, ALU.mult)
                ins.then_inc(dve_pe.tick(), 1)
                pe_done.wait(dve)
                cb = B[:, 32:35, :].rearrange("p a c -> p (a c)").rearrange("p (g c) -> p g c", g=2)
                for g in range(SSD_GROUPS):
                    tt(cb[:, g, 0:P], ps[2 + g][:, 0:P], tri, ALU.mult)
                    nc.vector.tensor_copy(cb[:, g, P:TOK], ps[2 + g][:, P:TOK])
                    ins = tt(cb[:, g, TOK:384], ps[2 + g][:, TOK:384], tri, ALU.mult)
                step(ins)
                for h in range(SSD_HEADS):
                    pe_done.wait(dve, 2 if h >= 3 and h % 2 else 1)
                    m = T[:, 4 + 2 * (h % 2):6 + 2 * (h % 2), :].rearrange("p a t -> p (a t)")[:, 0:384]
                    ts(m[:, 0:TOK], ps[h % 2][:, 0:TOK], cols[:, 2, h:h + 1], 0.0, ALU.subtract, ALU.min)
                    ts(m[:, TOK:384], ps[h % 2][:, P:TOK], cols[:, 3, h:h + 1], 0.0, ALU.subtract, ALU.min)\
                        .then_inc(dve_act.tick(), 1)
                    act_done.wait(dve)
                    tt(m, m, cb[:, h // 4, :], ALU.mult).then_inc(dve_pe.tick(), 1)
                pe_done.wait(dve)
                for p in range(4):
                    ins = stt(out=B[:, 36 + p, :], in0=B[:, 12 + p, :], scalar=V("d_skip", i * 4 + p),
                              in1=ps[4 + p][:, 0:TOK], op0=ALU.mult, op1=ALU.add)
                step(ins)
                step(tt(B[:, 44:48, :], B[:, 36:40, :], B[:, 40:44, :], ALU.mult))
                tt(B[:, 48:52, :], B[:, 44:48, :], B[:, 44:48, :], ALU.mult).then_inc(dve_pe.tick(), 1)
                step(tt(A[:, 18:20, :], A[:, 18:20, :], A[:, 20:22, :], ALU.mult))
                causal_conv(lambda k: A[:, 2 + k, :], lambda k: A[:, 18 + k, :], 2,
                            lambda k: COL["conf_conv"] + (i * 2 + k) * 32, CONF_KERNEL, True)\
                    .then_inc(dve_pe.tick(), 1)
                pe_done.wait(dve, 2)
                step(ts(MU[:, :], ps[1][:, 0:TOK], 1.0 / W_CONF, None, ALU.mult))
                step(tt(A[:, 2:4, :], A[:, 2:4, :], wide(MU[:, :], 2), ALU.subtract))
                tt(A[:, 4:6, :], A[:, 2:4, :], A[:, 2:4, :], ALU.mult).then_inc(dve_pe.tick(), 1)
                act_done.wait(dve)
                step(nc.vector.reciprocal(B[:, 52:54, :], B[:, 52:54, :]))
                for p in range(4):
                    ins = stt(out=B[:, 58 + p, :], in0=B[:, 44 + p, :], scalar=V("ssd_norm", i * 4 + p),
                              in1=B[:, 52 + p // 2, :], op0=ALU.mult, op1=ALU.mult)
                ins.then_inc(dve_pe.tick(), 1)
                pe_done.skip(dve, 1)
                act_done.wait(dve)
                step(nc.vector.reciprocal(R[:, 0, :], R[:, 0, :]))
                tt(A[:, 2:4, :], A[:, 2:4, :], wide(R[:, 0, :], 2), ALU.mult).then_inc(dve_act.tick(), 1)
                residual(("hy_out", i), 1, False)

            def moe(_):
                lg, eq, one, two, l2, gt = [rt[:, n, :, :] for n in range(6)]
                m1, m2, pick = small[:, 32:34], small[:, 34:36], small[:, 36:38]
                prior = con[:, CONST["prior"]:CONST["prior"] + EXPERTS]
                prior = prior.rearrange("p (o e) -> p o e", o=1).to_broadcast([P, 2, EXPERTS])

                def each(col):
                    return col.rearrange("p (t o) -> p t o", o=1).to_broadcast([P, 2, EXPERTS])

                def best(hot, logits, top):
                    step(nc.vector.tensor_reduce(top, logits, AX_X, ALU.max))
                    step(tt(eq, logits, each(top), ALU.is_equal))
                    step(tt(eq, eq, prior, ALU.mult))
                    step(nc.vector.tensor_reduce(pick, eq, AX_X, ALU.max))
                    step(tt(hot, eq, each(pick), ALU.is_equal))

                nc.vector.memset(B[:, 0, :], 0.0)
                pe_done.wait(dve)
                step(nc.vector.tensor_copy(lg, ps[4][:, 0:16].rearrange("p (t e) -> p t e", t=2)))
                best(one, lg, m1)
                step(stt(out=l2, in0=one, scalar=NEG, in1=lg, op0=ALU.mult, op1=ALU.add))
                best(two, l2, m2)
                tt(small[:, 38:40], m2, m1, ALU.subtract).then_inc(dve_act.tick(), 1)
                act_done.wait(dve)
                step(ts(small[:, 42:44], small[:, 40:42], 1.0, None, ALU.add))
                step(nc.vector.reciprocal(small[:, 42:44], small[:, 42:44]))
                step(tt(small[:, 44:46], small[:, 40:42], small[:, 42:44], ALU.mult))
                tt(one, one, each(small[:, 42:44]), ALU.mult)
                step(tt(two, two, each(small[:, 44:46]), ALU.mult))
                tt(B[:, 0, :].rearrange("p (t c) -> p t c", t=2)[:, :, 0:EXPERTS], one, two, ALU.add)\
                    .then_inc(dve_pe.tick(), 1)
                pe_done.skip(dve, 2)
                act_done.wait(dve)
                nu, nd = SLABS["moe_up"][0], SLABS["moe_down"][0]
                f0, s0 = before[("moe_up", 0)]["dve"], silu_done.now(dve)
                g0 = first_slab[("moe_down", 0)]
                with dve.Fori(0, EXPERTS) as e:
                    with dve.Fori(0, nu // 4) as i:
                        for b in range(4):
                            dve.wait_ge(silu_done.sem, e * nu + i * 4 + (s0 + b + 1))
                            tt(A[:, bass.ds(i * 4 + b, 1), :].rearrange("p a t -> p (a t)"), C[:, b, 0, :],
                               ps[b][:, TOK:512], ALU.mult).then_inc(free_dve, 1)
                    for m in range(4):
                        dve.wait_ge(slab_done, e * (nu + nd) + (g0 + 4 * (m + 1)))
                        t = T[:, 2 * m:2 * m + 2, :]
                        tt(t, ps[m % 2][:, :].rearrange("p (a t) -> p a t", a=2),
                           GB[:, bass.ds(e, 1), :].to_broadcast([P, 2, TOK]), ALU.mult).then_inc(free_dve, 1)
                        dve.wait_ge(free_dve, e * (nu + 4) + (f0 + nu + m + 1))
                        ins = tt(X[:, 2 * m:2 * m + 2, :], X[:, 2 * m:2 * m + 2, :], t, ALU.add)
                    ins.then_inc(moe_sum, 1)
                dve.wait_ge(moe_sum, EXPERTS)

            nc.vector.memset(eps[:, 0:1], EPS).then_inc(eps_ready, 1)
            nc.vector.memset(eps[:, 1:2], EPS_2).then_inc(eps_ready, 1)
            for b in range(CREDIT):
                nc.vector.memset(small[:, 48 + b:49 + b], 0.0).then_inc(free_act, 1)
                nc.vector.memset(small[:, 56 + b:57 + b], 0.0).then_inc(free_dve, 1)
            in_ready.wait(dve, 80)
            run({"norm": norm, "ada": ada, "gmlp": gmlp, "ffn": ffn, "mla": mla, "hgrn": hgrn,
                 "hybrid": hybrid, "swiglu": swiglu, "moe": moe})


def columns(v):
    v = np.ascontiguousarray(v).reshape(-1, P)
    return v.T


def pairs(w):
    n = w.shape[1] // 256
    return w.reshape(KD, P, n, 256).transpose(2, 1, 0, 3).reshape(n, P, KD * 256)


def gate_and_value(w):
    k, n = w.shape
    return w.reshape(k, 2, n // 256, P).transpose(0, 2, 1, 3).reshape(k, n)


def deep(w, tiles):
    parts = w.shape[0] // P // tiles
    return w.reshape(parts, tiles, P, 8, P).transpose(3, 0, 2, 1, 4).reshape(8 * parts, P, tiles * P)


def lay_out(v):
    f = {k: np.asarray(a) for k, a in v.items()}

    def zeros(*shape):
        return np.zeros(shape, np.float32)

    a = {}
    a["w_ada"] = np.concatenate([pairs(w) for w in f["ada_w"]])
    a["w_gm_in"] = np.concatenate([pairs(w) for w in f["gm_w_in"]])
    a["w_gm_out"] = np.concatenate([deep(w, 16) for w in f["gm_w_out"]])
    w = f["mla_w_a"][0]
    r1, r2, z = w[:, 384:416], w[:, 416:448], zeros(D, 64)
    a["w_mla_a"] = pairs(np.concatenate([w[:, :384], r1, r2, z, r2, r1, z, zeros(D, P)], 1))
    w = f["mla_w_qb"][0].reshape(Q_RANK, HEADS, NOPE + ROPE)
    r1, r2, z = w[:, :, 128:160], w[:, :, 160:192], zeros(Q_RANK, HEADS, 64)
    w = np.stack([w[:, :, :128], np.concatenate([r1, r2, z], 2), np.concatenate([r2, r1, z], 2)], 1)
    a["w_mla_qb"] = w.reshape(2, P, 3, 4, 2, P).transpose(2, 1, 3, 0, 4, 5).reshape(3, P, 16 * P)
    w = f["mla_w_kvb"][0].reshape(KV_RANK, HEADS, 2, 128).transpose(0, 2, 1, 3)
    a["w_mla_kvb"] = w.reshape(1, P, 16 * P)
    a["w_mla_o"] = pairs(f["mla_w_o"][0])
    w = f["hg_w_in"][0]
    a["w_hg_in"] = pairs(np.concatenate([w[:, :2048], w[:, 3072:], w[:, 2048:3072]], 1))
    a["w_hg_o"] = pairs(f["hg_w_o"][0])
    a["w_ff_up"] = np.concatenate([pairs(gate_and_value(w)) for w in f["ff_w_up"]])
    a["w_ff_down"] = np.concatenate([deep(w, KF // 2) for w in f["ff_w_down"]])
    hy = []
    for w in f["w_in_2"]:
        hy.append(pairs(np.concatenate([w[:, :2304], w[:, 2312:], w[:, 2304:2312], zeros(D, 120), zeros(D, P)], 1)))
    a["w_hy_in"] = np.concatenate(hy)
    a["w_hy_out"] = np.concatenate([pairs(w) for w in f["w_out_2"]])
    a["w_sw_up"] = pairs(gate_and_value(np.concatenate([f["ffn_w_gate_2"][0], f["ffn_w_up_2"][0]], 1)))
    a["w_sw_down"] = deep(f["ffn_w_down_2"][0], KF // 2)
    a["w_moe_up"] = np.concatenate([pairs(gate_and_value(np.concatenate([g, u], 1)))
                                    for g, u in zip(f["moe_w_gate_2"][0], f["moe_w_up_2"][0])])
    a["w_moe_down"] = np.concatenate([deep(w, KE // 2) for w in f["moe_w_down_2"][0]])

    freq = (ROPE_THETA ** (-np.arange(0, ROPE, 2, dtype=np.float32) / ROPE)).astype(np.float32)
    half = ROPE // 2

    def taps(w, b, tiles):
        rows = [w] if b is None else [w, b[None]]
        w = np.concatenate(rows)
        return w.reshape(w.shape[0], tiles, P).transpose(2, 1, 0).reshape(P, -1)

    def padded(x):
        return np.concatenate([x, zeros(P - SSD_HEADS)]).reshape(P, 1)

    ff = []
    for w, b in zip(f["ff_conv_w"], f["ff_conv_b"]):
        w = np.concatenate([w, b[None]]).reshape(4, 2, KF, P).transpose(3, 2, 1, 0)
        ff.append(w.reshape(P, KF * 8))
    vectors = {
        "c": columns(f["c"]), "ada_b": columns(f["ada_b"]), "mix_g": columns(f["mix_norm_g"]),
        "ffn_g": columns(f["ffn_norm_g"]), "gm_ln_g": columns(f["gm_ln_g"]), "gm_ln_b": columns(f["gm_ln_b"]),
        "q_norm": columns(f["mla_q_norm_g"]), "kv_norm": columns(f["mla_kv_norm_g"]),
        "hg_lb": columns(f["hg_lb"]), "hg_norm": columns(f["hg_norm_g"]), "ff_conv": np.concatenate(ff, 1),
        "final_g": columns(f["final_g"]), "norm_mix_2": columns(f["norm_mix_2"]),
        "conv_a": np.concatenate([taps(w, None, 2) for w in f["conv_a_w_2"]], 1),
        "conv_ssd": np.concatenate([taps(w, b, 8) for w, b in zip(f["conv_ssd_w_2"], f["conv_ssd_b_2"])], 1),
        "dt_bias": np.concatenate([padded(x) for x in f["dt_bias_2"]], 1),
        "a_log": np.concatenate([padded(x) for x in f["a_log_2"]], 1),
        "d_skip": columns(np.repeat(f["d_skip_2"], 64, axis=1)),
        "ssd_norm": columns(f["ssd_norm_w_2"]),
        "conf_conv": np.concatenate([taps(w, b, 2) for w, b in zip(f["conv_conf_w_2"], f["conv_conf_b_2"])], 1),
        "conf_ln_g": columns(f["conf_ln_g_2"]), "conf_ln_b": columns(f["conf_ln_b_2"]),
        "norm_ffn_2": columns(f["norm_ffn_2"]), "norm_final_2": columns(f["norm_final_2"]),
        "inv_freq": np.concatenate([freq, freq, zeros(64)]).reshape(P, 1),
        "rope_sign": np.concatenate([-np.ones(half), np.ones(half), np.zeros(64)]).astype(np.float32).reshape(P, 1),
        "router": f["moe_router_2"][0].reshape(KD, P, EXPERTS).transpose(1, 0, 2).reshape(P, KD * EXPERTS),
    }
    assert [(n, COL[n]) for n in vectors] == list(COL.items())
    a["vectors"] = np.concatenate(list(vectors.values()), 1)

    s, t = np.arange(P)[:, None], np.arange(P)[None, :]
    blocks = [(s // (2 * L) == t // (2 * L)) & (s // L % 2 == 0) & (t // L % 2 == 1) for L in LEVELS[1:]]
    blocks += [s == t, s == t, s <= t, np.where(t <= s, 0.0, NEG), np.ones((P, TOK))]
    blocks += [np.broadcast_to(s == e, (P, P)) for e in range(8)]
    blocks += [np.broadcast_to(EXPERTS - np.arange(EXPERTS), (P, EXPERTS))]
    a["constants"] = np.concatenate([b.astype(np.float32) for b in blocks], 1)

    ws = f["gm_w_s"].transpose(0, 3, 1, 2).reshape(2, P, GM_GROUPS * P)
    bs = np.broadcast_to(f["gm_b_s"].reshape(2, 1, GM_GROUPS * P), (2, P, GM_GROUPS * P))
    a["spatial"] = np.concatenate([ws, bs], 2).transpose(1, 0, 2)
    a["x"] = f["x"][0].reshape(TOK, KD, P).transpose(2, 1, 0)
    a["positions"] = np.broadcast_to(f["positions"][0], (P, TOK))
    return {k: np.ascontiguousarray(x) for k, x in a.items()}


def kernel(**inputs):
    import numpy as _np
    import concourse.bacc as _bacc
    from concourse import mybir as _mybir
    from concourse.bass_utils import run_bass_kernel_spmd as _run

    nc = _bacc.Bacc("TRN2", target_bir_lowering=False, num_devices=1)
    arrays = lay_out(inputs)
    ins = {k: nc.dram_tensor(k, x.shape, _mybir.dt.from_np(x.dtype), kind="ExternalInput").ap()
           for k, x in arrays.items()}
    out = nc.dram_tensor("out", (P, KD, TOK), _mybir.dt.float32, kind="ExternalOutput").ap()
    build(nc, ins, out)
    r = _run(nc, [arrays], core_ids=[0])
    got = r.results[0]["out"]
    return _np.ascontiguousarray(got.transpose(2, 1, 0)).reshape(1, TOK, D)
```

```python
from contextlib import ExitStack

import concourse.bass as bass
from concourse import mybir
import numpy as np

F32 = mybir.dt.float32
I32 = mybir.dt.int32
ALU = mybir.AluOpType
ACT = mybir.ActivationFunctionType
AX_X = mybir.AxisListType.X

P = 128
TOK = 256
D = 1024
KD = D // P
DEPTH, DEPTH_2 = 4, 2
EPS, EPS_2 = 1e-6, 1e-5
FF = 2816
KF = FF // P
GM_INNER, GM_GROUPS = 2048, 8
KG = GM_INNER // P
HEADS = 8
Q_RANK, KV_RANK, NOPE, ROPE = 256, 128, 128, 64
ATT_SCALE = float((NOPE + ROPE) ** -0.5)
ROPE_THETA = 10000.0
W_A, W_SSD, W_CONF = 256, 512, 256
SSD_HEADS, SSD_GROUPS = 8, 2
CONF_KERNEL = 31
EXPERTS, EF = 8, 3584
KE = EF // P
SLOTS = P
PASSES = EXPERTS + (2 * TOK) // (SLOTS + 1)
LEVELS = [128, 64, 32, 16, 8, 4, 2, 1]
NEG = -1e30

RING = 4
SLAB_TILES = 16

ADA_SLABS = DEPTH * 6 * D // 256
ADA_ACT = 6

SLABS = {
    "ada": (6 * D // 256, 16), "gm_in": (2 * GM_INNER // 256, 16), "gm_out": (8, 16),
    "mla_a": (3, 16), "mla_qb": (3, 16), "mla_kvb": (1, 16), "mla_o": (4, 16),
    "hg_in": (16, 16), "hg_o": (4, 16), "ff_up": (KF, 16), "ff_down": (16, KF // 2),
    "hy_in": (12, 16), "hy_out": (4, 16), "sw_up": (KF, 16), "sw_down": (16, KF // 2),
    "moe_up": (KE, 16), "moe_down": (16, KE // 2),
}


def program_order(stages):
    out = []
    for kind, i in stages:
        if kind == "ada":
            out += [("ada", n) for n in range(DEPTH)]
        elif kind == "gmlp":
            out += [("gm_in", i // 3), ("gm_out", i // 3)]
        elif kind == "mla":
            out += [("mla_a", 0), ("mla_qb", 0), ("mla_kvb", 0), ("mla_o", 0)]
        elif kind == "hgrn":
            out += [("hg_in", 0), ("hg_o", 0)]
        elif kind == "ffn":
            out += [("ff_up", i), ("ff_down", i)]
        elif kind == "hybrid":
            out += [("hy_in", i), ("hy_out", i)]
        elif kind == "swiglu":
            out += [("sw_up", 0), ("sw_down", 0)]
        elif kind == "moe":
            for e in range(EXPERTS):
                out += [("moe_up", e), ("moe_down", e)]
    return out


STAGES = [("ada", 0), ("gmlp", 0), ("ffn", 0), ("mla", 1), ("ffn", 1), ("hgrn", 2), ("ffn", 2),
          ("gmlp", 3), ("ffn", 3), ("final_1", 0),
          ("hybrid", 0), ("swiglu", 0), ("hybrid", 1), ("moe", 1), ("final_2", 0)]


def column_layout():
    at, n = {}, 0
    for name, cols in [
        ("c", KD), ("ada_b", DEPTH * 48), ("mix_g", DEPTH * KD), ("ffn_g", DEPTH * KD),
        ("gm_ln_g", 2 * KG), ("gm_ln_b", 2 * KG), ("q_norm", 2), ("kv_norm", 1), ("hg_lb", DEPTH * KD),
        ("hg_norm", 1), ("ff_conv", DEPTH * KF * 8), ("final_g", KD), ("norm_mix_2", 2 * KD),
        ("conv_a", 2 * 2 * 3), ("conv_ssd", 2 * 8 * 5), ("dt_bias", 2), ("a_log", 2), ("d_skip", 2 * 4),
        ("ssd_norm", 2 * 4), ("conf_conv", 2 * 2 * 32), ("conf_ln_g", 2 * 2), ("conf_ln_b", 2 * 2),
        ("norm_ffn_2", 2 * KD), ("norm_final_2", KD), ("inv_freq", 1), ("rope_sign", 1),
        ("router", KD * EXPERTS),
    ]:
        at[name] = n
        n += cols
    return at, n


COL, NCOL = column_layout()
CONST = {"mask": 0, "ident": 8 * P, "tri": 9 * P, "neg": 10 * P, "ones": 11 * P, "sel": 13 * P,
         "iota": 21 * P, "prior": 22 * P, "expert": 22 * P + 8}
NCONST = 22 * P + 16


class Count:

    def __init__(self, sem):
        self.sem = sem
        self.seen = {}
        self.made = 0

    def tick(self):
        self.made += 1
        return self.sem

    def own(self, eng):
        eng.wait_ge(self.sem, self.made)

    def wait(self, eng, n=1):
        self.seen[eng] = self.seen.get(eng, 0) + n
        eng.wait_ge(self.sem, self.seen[eng])

    def now(self, eng):
        return self.seen.get(eng, 0)

    def skip(self, eng, n):
        self.seen[eng] = self.seen.get(eng, 0) + n


def build(nc, ins, out, stages=STAGES):
    order = program_order(stages)
    first_slab, n = {}, 0
    for sec in order:
        first_slab[sec] = n
        n += SLABS[sec[0]][0]

    with ExitStack() as ctx:
        def sb(name, shape, dt=F32):
            return ctx.enter_context(nc.sbuf_tensor(name, shape, dt))

        def sem(name):
            return ctx.enter_context(nc.semaphore(name))

        ring = sb("ring", [P, RING, SLAB_TILES * P])
        X = sb("X", [P, KD, TOK])
        H = sb("H", [P, KD, TOK])
        T = sb("T", [P, KD, TOK])
        C = sb("C", [P, 4, 2, TOK])
        A = sb("A", [P, 32, TOK])
        B = sb("B", [P, 64, TOK])
        R = sb("R", [P, 2, TOK])
        MU = sb("MU", [P, TOK])
        posi = sb("posi", [P, TOK], I32)
        rt = sb("rt", [P, 6, 2, EXPERTS])
        vec = sb("vec", [P, NCOL])
        con = sb("con", [P, NCONST])
        mod = sb("mod", [P, DEPTH * 48])
        cact = sb("cact", [P, KD])
        acol = sb("acol", [P, KD])
        gcol = sb("gcol", [P, KD])
        eps = sb("eps", [P, 2])
        wsbs = sb("wsbs", [P, 2, 2 * GM_GROUPS * P])
        small = sb("small", [P, 64])
        lbs = sb("lbs", [P, 6, KD])
        passes = sb("passes", [P, 3, 2, PASSES + 1])
        plan = sb("plan", [P, PASSES + 1])
        plan_i = sb("plan_i", [P, PASSES + 1], I32)
        ps = [ctx.enter_context(nc.psum_tensor(f"ps{i}", [P, 512], F32)) for i in range(8)]

        ident = con[:, CONST["ident"]:CONST["ident"] + P]
        tri = con[:, CONST["tri"]:CONST["tri"] + P]
        negm = con[:, CONST["neg"]:CONST["neg"] + P]
        ones = con[:, CONST["ones"]:CONST["ones"] + P]
        ones_wide = con[:, CONST["ones"]:CONST["ones"] + TOK]

        def V(name, i=0, n=1):
            return vec[:, COL[name] + i:COL[name] + i + n]

        def sel(h):
            return con[:, CONST["sel"] + h * P:CONST["sel"] + (h + 1) * P]

        w_ready = [sem(f"w_ready{b}") for b in range(RING)]
        vec_ready = sem("vec_ready")
        con_ready = sem("con_ready")
        in_ready = sem("in_ready")
        out_done = sem("out_done")
        slab_done = sem("slab_done")
        pe_done = Count(sem("pe_done"))
        free_act = sem("free_act")
        free_dve = sem("free_dve")
        act_step = Count(sem("act_step"))
        dve_step = Count(sem("dve_step"))
        act_done = Count(sem("act_done"))
        act_pe = Count(sem("act_pe"))
        dve_act = Count(sem("dve_act"))
        dve_pe = Count(sem("dve_pe"))
        h_ready = Count(sem("h_ready"))
        silu_done = Count(sem("silu_done"))
        g_ready = Count(sem("g_ready"))
        act_conv = sem("act_conv")
        conv_step = sem("conv_step")
        plan_ready = sem("plan_ready")
        dve_moe = sem("dve_moe")
        pe_moe = sem("pe_moe")
        act_moe = sem("act_moe")
        dve_add = sem("dve_add")
        eps_ready = sem("eps_ready")
        ada_scaled = sem("ada_scaled")
        ada_own = sem("ada_own")
        ada_sum = sem("ada_sum")

        CREDIT = 4
        freed = {"act": CREDIT, "dve": CREDIT}

        def norm_of(kind, i):
            if kind == "final_1":
                return 0, None, X, COL["final_g"], None, None
            if kind == "final_2":
                return 1, None, H, COL["norm_final_2"], None, None
            if kind in ("hybrid", "swiglu", "moe"):
                return 1, None, H, COL["norm_mix_2" if kind == "hybrid" else "norm_ffn_2"] + i * KD, None, None
            m = i * 48 + (24 if kind == "ffn" else 0)
            return 0, m, H, COL["ffn_g" if kind == "ffn" else "mix_g"] + i * KD, m + KD, m + 2 * KD

        def run(do):
            for kind, i in stages:
                if kind != "ada":
                    do["norm"](norm_of(kind, i))
                if not kind.startswith("final"):
                    do[kind](i)

        h_tok = B[:, 8:16, :].rearrange("p (t a) c -> p t (a c)", t=2)
        hg = B[:, 16:20, :].rearrange("p a (r c) -> p (a r) c", c=SLOTS)
        place, gplace, gplace_t = B[:, 20, :], B[:, 21, :], B[:, 22, :]
        y_slot = B[:, 24:28, :].rearrange("p a c -> p (a c)")
        nu, nd = SLABS["moe_up"][0], SLABS["moe_down"][0]
        SPP = nu + nd
        EV_PE, EV_ACT, EV_ADD = 6, 4, 4

        h_total = KD * sum(norm_of(kind, i)[2] is H for kind, i in stages if kind != "ada")
        block = ctx.enter_context(nc.Block())

        def bank_uses(name):
            n = SLABS[name][0]
            who = {"gm_in": "act", "mla_a": "act", "mla_qb": "act", "mla_kvb": "act", "hg_in": "act",
                   "hy_in": "act"}.get(name, "dve")
            banks = {"ada": 0, "gm_out": 4, "ff_down": 4, "sw_down": 4, "moe_down": 4, "mla_qb": 12,
                     "mla_kvb": 8}.get(name, n)
            return banks, who

        before, total = {}, dict(freed)
        for sec in order:
            before[sec] = dict(total)
            banks, who = bank_uses(sec[0])
            total[who] += banks
            if sec[0] == "hg_in":
                total["act"] += 4

        @block.sync
        def _(sp):
            sp.dma_start(vec[:, :], ins["vectors"]).then_inc(vec_ready, 16)

            for name, use in order:
                if name.startswith("moe") and use > 0:
                    continue
                n, tiles = SLABS[name]
                g0 = first_slab[(name, use)]
                src = ins["w_" + name]
                if name == "moe_down":
                    continue
                if name == "moe_up":
                    td = SLABS["moe_down"][1]
                    sp.wait_ge(plan_ready, 1)
                    count = sp.value_load(plan_i[0:1, PASSES:PASSES + 1], min_val=EXPERTS, max_val=PASSES)
                    with sp.Fori(0, count) as p:
                        e = sp.value_load(plan_i[0:1, bass.ds(p, 1)], min_val=0, max_val=EXPERTS - 1)
                        with sp.Fori(0, nu // RING) as i:
                            for b in range(RING):
                                sp.wait_ge(slab_done, p * SPP + i * RING + (g0 + b - RING + 1))
                                sp.dma_start(ring[:, (g0 + b) % RING, 0:tiles * P],
                                             src[e * nu + i * RING + b]).then_inc(w_ready[(g0 + b) % RING], 16)
                        with sp.Fori(0, nd // RING) as i:
                            for b in range(RING):
                                sp.wait_ge(slab_done, p * SPP + i * RING + (g0 + nu + b - RING + 1))
                                sp.dma_start(ring[:, (g0 + nu + b) % RING, 0:td * P],
                                             ins["w_moe_down"][e * nd + i * RING + b])\
                                  .then_inc(w_ready[(g0 + nu + b) % RING], 16)
                    continue
                s = 0
                if g0 == 0:
                    for b in range(RING):
                        sp.dma_start(ring[:, b, 0:tiles * P], src[use * n + b]).then_inc(w_ready[b], 16)
                    sp.dma_start(con[:, :], ins["constants"]).then_inc(con_ready, 16)
                    sp.dma_start(X[:, :, :], ins["x"]).then_inc(in_ready, 16)
                    sp.dma_start(wsbs[:, :, :], ins["spatial"]).then_inc(in_ready, 16)
                    sp.dma_start(posi[:, :], ins["positions"]).then_inc(in_ready, 16)
                    s = RING
                rounds = (n - s) // RING
                if rounds > 1:
                    with sp.Fori(0, rounds) as i:
                        for b in range(RING):
                            g = g0 + s + b
                            sp.wait_ge(slab_done, i * RING + (g - RING + 1))
                            sp.dma_start(ring[:, g % RING, 0:tiles * P],
                                         src[i * RING + (use * n + s + b)]).then_inc(w_ready[g % RING], 16)
                    s += rounds * RING
                for t in range(s, n):
                    g = g0 + t
                    sp.wait_ge(slab_done, g - RING + 1)
                    sp.dma_start(ring[:, g % RING, 0:tiles * P], src[use * n + t])\
                      .then_inc(w_ready[g % RING], 16)
            h_ready.wait(sp, h_total)
            sp.dma_start(out, H[:, :, :]).then_inc(out_done, 16)
            sp.wait_ge(out_done, 16)

        @block.tensor
        def _(pe):
            mm = nc.tensor.matmul

            def slab_wait(g, r=0):
                pe.wait_ge(w_ready[g % RING], r * 16 + 16 * (g // RING + 1))

            def banks_back(sec):
                pe.wait_ge(free_act, before[sec]["act"])
                pe.wait_ge(free_dve, before[sec]["dve"])

            def bank_wait(sec, m, r=0):
                _, who = bank_uses(sec[0])
                pe.wait_ge({"act": free_act, "dve": free_dve}[who], r + (before[sec][who] + m - 3))

            def pair(bank, slot, src, n=TOK):
                for j in range(2):
                    for k in range(KD):
                        last = mm(bank[:, j * n:(j + 1) * n], ring[:, slot, k * 256 + j * P:k * 256 + j * P + P],
                                  src[:, k, :], start=(k == 0), stop=(k == KD - 1))
                return last

            def gemm(sec, src, n=TOK, slabs=None):
                g0 = first_slab[sec]
                count = slabs or SLABS[sec[0]][0]
                banks_back(sec)
                rounds = count // 4
                s = 0
                if rounds > 1:
                    with pe.Fori(0, rounds) as i:
                        for b in range(4):
                            slab_wait(g0 + b, i)
                            bank_wait(sec, b, i * 4)
                            pair(ps[b], (g0 + b) % RING, src, n).then_inc(slab_done, 1)
                    s = rounds * 4
                for t in range(s, count):
                    slab_wait(g0 + t)
                    bank_wait(sec, t)
                    pair(ps[t % 4], (g0 + t) % RING, src, n).then_inc(slab_done, 1)

            def deep_body(sec, src, i, kt, per_tile, r0):
                g0 = first_slab[sec]
                per_slab = kt // per_tile
                s = 0
                for m in range(2):
                    pe.wait_ge(free_dve, i * 2 + r0[0] + (before[sec]["dve"] + m - 1))
                    for j in range(2):
                        for part in range(per_tile):
                            g = g0 + s
                            pe.wait_ge(w_ready[g % RING], i * (16 * per_tile) + r0[1] + 16 * (g // RING + 1))
                            for k in range(per_slab):
                                kk = part * per_slab + k
                                last = mm(ps[m][:, j * TOK:(j + 1) * TOK],
                                          ring[:, g % RING, k * P:(k + 1) * P], src[:, kk, :],
                                          start=(kk == 0), stop=(kk == kt - 1))
                            last.then_inc(slab_done, 1)
                            s += 1

            def gemm_deep(sec, src, kt, per_tile):
                banks_back(sec)
                with pe.Fori(0, 2) as i:
                    deep_body(sec, src, i, kt, per_tile, (0, 0))

            def stat(dst, tiles):
                for k, t in enumerate(tiles):
                    last = mm(dst, ones, t, start=(k == 0), stop=(k == len(tiles) - 1))
                return last

            def norm(_):
                for k in range(KD):
                    if k % 2 == 0:
                        dve_pe.wait(pe)
                    last = mm(ps[4][:, 0:TOK], ones, T[:, k, :], start=(k == 0), stop=(k == KD - 1))
                last.then_inc(pe_done.sem, 1)

            def ada(_):
                with pe.Fori(0, ADA_SLABS // 4) as i:
                    for b in range(4):
                        pe.wait_ge(ada_sum, i * 4 + (b + 1))
                        for j in range(2):
                            last = mm(ps[4][:, bass.ds(i * 8 + (2 * b + j), 1)], C[:, b, 0, j * P:(j + 1) * P],
                                      ones[:, 0:1], start=True, stop=True)
                        last.then_inc(slab_done, 1)
                pe.wait_ge(in_ready, 48)

            def gmlp(i):
                j = i // 3
                h_ready.wait(pe, KD)
                gemm(("gm_in", j), H)
                pe.wait_ge(free_act, before[("gm_out", j)]["act"])
                stat(ps[4][:, 0:TOK], [A[:, KG + k, :] for k in range(KG)]).then_inc(pe_done.sem, 1)
                dve_pe.wait(pe)
                stat(ps[4][:, 256:512], [B[:, k, :] for k in range(KG)]).then_inc(pe_done.sem, 1)
                for q in range(KG // 2):
                    act_pe.wait(pe)
                    if q >= 2:
                        act_pe.wait(pe)
                    for k in range(2):
                        for c in range(2):
                            last = nc.tensor.transpose(ps[4 + q % 2][:, (2 * k + c) * P:(2 * k + c + 1) * P],
                                                       A[:, KG + 2 * q + k, c * P:(c + 1) * P], ident)
                    last.then_inc(pe_done.sem, 1)
                act_pe.wait(pe, 2)
                for q in range(KG // 2):
                    if q >= 2:
                        dve_pe.wait(pe)
                    for k in range(2):
                        for c in range(2):
                            last = mm(ps[6 + q % 2][:, (2 * k + c) * P:(2 * k + c + 1) * P],
                                      B[:, 16 + 2 * q + k, c * P:(c + 1) * P],
                                      wsbs[:, j, q * P:(q + 1) * P], start=True, stop=True)
                    last.then_inc(pe_done.sem, 1)
                dve_pe.wait(pe, 2)
                gemm_deep(("gm_out", j), A, KG, 1)

            def ffn(i):
                h_ready.wait(pe, KD)
                gemm(("ff_up", i), H)
                g_ready.wait(pe, KF)
                gemm_deep(("ff_down", i), A, KF, 2)

            def swiglu(_):
                h_ready.wait(pe, KD)
                gemm(("sw_up", 0), H)
                pe.wait_ge(free_dve, before[("sw_down", 0)]["dve"])
                gemm_deep(("sw_down", 0), A, KF, 2)

            def mla(i):
                h_ready.wait(pe, KD)
                gemm(("mla_a", 0), H)
                dve_pe.wait(pe)
                stat(ps[4][:, 0:TOK], [B[:, 0, :], B[:, 1, :]])
                stat(ps[4][:, 256:512], [B[:, 2, :]]).then_inc(pe_done.sem, 1)
                dve_pe.wait(pe)
                sec = ("mla_qb", 0)
                banks_back(sec)
                for s in range(3):
                    g = first_slab[sec] + s
                    slab_wait(g)
                    for b in range(4):
                        bank_wait(sec, 4 * s + b)
                        for j in range(2):
                            for k in range(2):
                                o = (4 * b + 2 * k + j) * P
                                last = mm(ps[b][:, j * TOK:(j + 1) * TOK], ring[:, g % RING, o:o + P],
                                          A[:, k, :], start=(k == 0), stop=(k == 1))
                        last.then_inc(slab_done if b == 3 else pe_done.sem, 1)
                sec = ("mla_kvb", 0)
                g = first_slab[sec]
                slab_wait(g)
                banks_back(sec)
                for b in range(4):
                    bank_wait(sec, b)
                    for j in range(2):
                        o = (2 * b + j) * P
                        last = mm(ps[b][:, j * TOK:(j + 1) * TOK], ring[:, g % RING, o:o + P], A[:, 2, :],
                                  start=True, stop=True)
                    last.then_inc(pe_done.sem, 1)
                for b in range(4):
                    bank_wait(sec, 4 + b)
                    t, half = b // 2, b % 2
                    last = mm(ps[b][:, :], A[:, 2, t * P:(t + 1) * P],
                              ring[:, g % RING, 1024 + half * 512:1024 + half * 512 + 512], start=True, stop=True)
                    last.then_inc(slab_done if b == 3 else pe_done.sem, 1)
                pe.wait_ge(free_act, before[("mla_o", 0)]["act"])
                dve_pe.wait(pe)

                def scores(h):
                    for q, (lo, hi) in enumerate([(0, P), (P, 384)]):
                        n = hi - lo
                        mm(ps[h % 2][:, lo:hi], B[:, 8 + h, q * P:(q + 1) * P], A[:, 8 + h, 0:n],
                           start=True, stop=False)
                        last = mm(ps[h % 2][:, lo:hi], B[:, 16 + h, q * P:(q + 1) * P], A[:, 3, 0:n],
                                  start=False, stop=True)
                    last.then_inc(pe_done.sem, 1)

                scores(0)
                for h in range(HEADS):
                    if h + 1 < HEADS:
                        scores(h + 1)
                    dve_pe.wait(pe)
                    for n in range(3):
                        last = nc.tensor.transpose(ps[2 + h % 2][:, n * P:(n + 1) * P],
                                                   T[:, 2 * (h % 2):2 * (h % 2) + 2, :]
                                                   .rearrange("p a t -> p (a t)")[:, n * P:(n + 1) * P], ident)
                    last.then_inc(pe_done.sem, 1)
                    act_pe.wait(pe, 2 if h else 1)
                    pt = T[:, 4 + 2 * (h % 2):6 + 2 * (h % 2), :].rearrange("p a t -> p (a t)")
                    v = B[:, 32:40, :].rearrange("p (t a) c -> p t (a c)", t=2)
                    mm(ps[4 + h % 2][:, 0:TOK], v[:, 0, h * P:(h + 1) * P], pt[:, 0:256], start=True, stop=False)
                    mm(ps[4 + h % 2][:, P:TOK], v[:, 1, h * P:(h + 1) * P], pt[:, 256:384], start=False, stop=True)\
                        .then_inc(pe_done.sem, 1)
                act_pe.wait(pe)
                gemm(("mla_o", 0), B[:, 40:48, :])

            def hgrn(i):
                h_ready.wait(pe, KD)
                sec = ("hg_in", 0)
                gemm(sec, H, slabs=12)
                g0 = first_slab[sec] + 12
                for b in range(4):
                    slab_wait(g0 + b)
                    bank_wait(sec, 12 + b)
                    for t in range(2):
                        for k in range(KD):
                            last = mm(ps[b][:, t * TOK:(t + 1) * TOK], H[:, k, t * P:(t + 1) * P],
                                      ring[:, (g0 + b) % RING, k * 256:(k + 1) * 256],
                                      start=(k == 0), stop=(k == KD - 1))
                    last.then_inc(slab_done, 1)
                for n, L in enumerate(LEVELS + [0]):
                    if L:
                        dve_pe.wait(pe)
                    if n:
                        dve_pe.wait(pe)
                    for h in range(HEADS):
                        q, k = (B[:, 32 + h, :], B[:, 40 + h, :]) if L else (A[:, h, :], B[:, h, :])
                        if L == 128:
                            last = mm(ps[4 + h // 4][:, (h % 4) * P:(h % 4 + 1) * P], k[:, 0:P], q[:, P:TOK],
                                      start=True, stop=True)
                        else:
                            for t in range(2):
                                o = (h % 2) * TOK + t * P
                                last = mm(ps[4 + h // 2][:, o:o + P], k[:, t * P:(t + 1) * P],
                                          q[:, t * P:(t + 1) * P], start=True, stop=True)
                    last.then_inc(pe_done.sem, 1)
                dve_pe.wait(pe, 2)
                pe.wait_ge(free_act, before[("hg_in", 0)]["act"] + 16)
                iv = A[:, 24:32, :].rearrange("p (t a) c -> p t (a c)", t=2)
                att = B[:, 48:60, :].rearrange("p a c -> p (a c)").rearrange("p (h c) -> p h c", h=HEADS)
                for h in range(HEADS):
                    o = (h % 2) * TOK
                    mm(ps[h // 2][:, o:o + TOK], iv[:, 0, h * P:(h + 1) * P], att[:, h, 0:TOK],
                       start=True, stop=False)
                    last = mm(ps[h // 2][:, o + P:o + TOK], iv[:, 1, h * P:(h + 1) * P], att[:, h, TOK:384],
                              start=False, stop=True)
                    if h % 2:
                        last.then_inc(pe_done.sem, 1)
                dve_pe.wait(pe)
                for b in range(4):
                    last = mm(ps[4 + b][:, :], ones, B[:, 8 + 2 * b:10 + 2 * b, :], start=True, stop=True)
                last.then_inc(pe_done.sem, 1)
                dve_pe.wait(pe)
                gemm(("hg_o", 0), B[:, 32:40, :])

            def hybrid(i):
                h_ready.wait(pe, KD)
                gemm(("hy_in", i), H)
                dve_pe.wait(pe)
                for n in range(4):
                    last = nc.tensor.transpose(ps[4][:, n * P:(n + 1) * P],
                                               B[:, 20 + n // 2, (n % 2) * P:(n % 2 + 1) * P], ident)
                last.then_inc(pe_done.sem, 1)
                act_pe.wait(pe)
                for t in range(2):
                    for n in range(4):
                        last = nc.tensor.transpose(ps[5 + t][:, n * P:(n + 1) * P],
                                                   B[:, 12 + n, t * P:(t + 1) * P], ident)
                last.then_inc(pe_done.sem, 1)
                pe.wait_ge(free_act, before[("hy_out", i)]["act"])
                for g in range(SSD_GROUPS):
                    dst = ps[2 + g]
                    mm(dst[:, 0:TOK], B[:, 16 + g, 0:P], B[:, 18 + g, 0:TOK], start=True, stop=True)
                    last = mm(dst[:, TOK:384], B[:, 16 + g, P:TOK], B[:, 18 + g, P:TOK], start=True, stop=True)
                last.then_inc(pe_done.sem, 1)

                def spread(h):
                    mm(ps[h % 2][:, 0:TOK], sel(h), B[:, 21, :], start=True, stop=True).then_inc(pe_done.sem, 1)

                spread(0)
                dve_pe.wait(pe)
                for h in range(SSD_HEADS):
                    if h + 1 < SSD_HEADS:
                        spread(h + 1)
                    dve_pe.wait(pe)
                    m = T[:, 4 + 2 * (h % 2):6 + 2 * (h % 2), :].rearrange("p a t -> p (a t)")
                    xd = B[:, 24 + h, :]
                    y = ps[4 + h // 2]
                    mm(y[:, 0:TOK], xd[:, 0:P], m[:, 0:TOK], start=(h % 2 == 0), stop=False)
                    last = mm(y[:, P:TOK], xd[:, P:TOK], m[:, TOK:384], start=False, stop=(h % 2 == 1))
                    if h % 2:
                        last.then_inc(pe_done.sem, 1)
                dve_pe.wait(pe)
                for g in range(SSD_GROUPS):
                    last = stat(ps[0][:, g * TOK:(g + 1) * TOK], [B[:, 48 + 2 * g + k, :] for k in range(2)])
                last.then_inc(pe_done.sem, 1)
                dve_pe.wait(pe)
                stat(ps[1][:, 0:TOK], [A[:, 2 + k, :] for k in range(2)]).then_inc(pe_done.sem, 1)
                dve_pe.wait(pe)
                stat(ps[1][:, TOK:512], [A[:, 4 + k, :] for k in range(2)]).then_inc(pe_done.sem, 1)
                act_pe.wait(pe)
                dve_pe.wait(pe)
                gemm(("hy_out", i), B[:, 56:64, :])

            def moe(_):
                h_ready.wait(pe, KD)
                banks_back(("moe_up", 0))
                for t in range(2):
                    for k in range(KD):
                        last = mm(ps[4][:, t * 8:(t + 1) * 8], H[:, k, t * P:(t + 1) * P],
                                  V("router", k * EXPERTS, EXPERTS), start=(k == 0), stop=(k == KD - 1))
                last.then_inc(pe_done.sem, 1)
                for t in range(2):
                    for k in range(KD):
                        last = nc.tensor.transpose(ps[2 * t + k // 4][:, (k % 4) * P:(k % 4 + 1) * P],
                                                   H[:, k, t * P:(t + 1) * P], ident)
                last.then_inc(pe_done.sem, 1)
                dve_pe.wait(pe)
                chosen = [passes[:, 0, t, 0:EXPERTS] for t in range(2)]
                mm(ps[6][:, 0:8], tri, chosen[0], start=True, stop=True)
                mm(ps[6][:, 8:16], ones, chosen[0], start=True, stop=False)
                mm(ps[6][:, 8:16], tri, chosen[1], start=False, stop=True)
                mm(ps[6][:, 16:24], ones, chosen[0], start=True, stop=False)
                mm(ps[6][:, 16:24], ones, chosen[1], start=False, stop=True).then_inc(pe_done.sem, 1)
                act_pe.wait(pe)
                pe.wait_ge(dve_moe, 1)

                def gather():
                    for k in range(KD):
                        for t in range(2):
                            last = mm(ps[6 + k // 4][:, (k % 4) * SLOTS:(k % 4 + 1) * SLOTS],
                                      h_tok[:, t, k * P:(k + 1) * P], place[:, t * SLOTS:(t + 1) * SLOTS],
                                      start=(t == 0), stop=(t == 1))
                    last.then_inc(pe_moe, 1)

                gather()
                up, down = ("moe_up", 0), ("moe_down", 0)
                gu, gd, f0 = first_slab[up], first_slab[down], before[up]["dve"]
                pe.wait_ge(plan_ready, 1)
                count = pe.value_load(plan_i[0:1, PASSES:PASSES + 1], min_val=EXPERTS, max_val=PASSES)
                with pe.Fori(0, count) as p:
                    with pe.Fori(0, nu // 4) as i:
                        pe.wait_ge(act_moe, p * EV_ACT + 1)
                        for b in range(4):
                            pe.wait_ge(w_ready[(gu + b) % RING],
                                       p * (16 * SPP // RING) + i * 16 + 16 * ((gu + b) // RING + 1))
                            pe.wait_ge(free_dve, p * nu + i * 4 + (f0 + b - 3))
                            pair(ps[b], (gu + b) % RING, hg, SLOTS).then_inc(slab_done, 1)
                    pe.wait_ge(free_dve, p * nu + (f0 + nu))
                    pe.wait_ge(dve_moe, p + 2)
                    pe.wait_ge(dve_add, p * EV_ADD + 1)
                    gather()
                    for t in range(2):
                        last = nc.tensor.transpose(ps[5][:, 256 + t * P:256 + (t + 1) * P],
                                                   gplace[:, t * SLOTS:(t + 1) * SLOTS], ident)
                    last.then_inc(pe_moe, 1)
                    for q in range(4):
                        if q == 2:
                            pe.wait_ge(act_moe, p * EV_ACT + 3)
                        for part in range(4):
                            g = gd + 4 * q + part
                            pe.wait_ge(w_ready[g % RING], p * (16 * SPP // RING) + 16 * (g // RING + 1))
                            for k in range(KE // 4):
                                kk = part * (KE // 4) + k
                                last = mm(ps[4 + q // 2][:, (q % 2) * 256:(q % 2 + 1) * 256], A[:, kk, 0:SLOTS],
                                          ring[:, g % RING, k * 256:(k + 1) * 256],
                                          start=(kk == 0), stop=(kk == KE - 1))
                            last.then_inc(slab_done, 1)
                    pe.wait_ge(act_moe, p * EV_ACT + 5)
                    for m in range(4):
                        if m >= 2:
                            pe.wait_ge(dve_add, p * EV_ADD + m)
                        for j in range(2):
                            o = (2 * m + j) * P
                            last = mm(ps[6 + m % 2][:, j * TOK:(j + 1) * TOK], y_slot[:, o:o + P], gplace_t,
                                      start=True, stop=True)
                        last.then_inc(pe_moe, 1)

            pe.wait_ge(con_ready, 16)
            run({"norm": norm, "ada": ada, "gmlp": gmlp, "ffn": ffn, "mla": mla, "hgrn": hgrn,
                 "hybrid": hybrid, "swiglu": swiglu, "moe": moe})

        @block.scalar
        def _(act):
            af = nc.scalar.activation

            def step(ins):
                ins.then_inc(act_step.tick(), 1)
                act_step.own(act)

            def evac(sec, func, dst, count=None, m0=0):
                g0 = first_slab[sec] + m0
                count = count or SLABS[sec[0]][0]
                rounds = count // 4
                s = 0
                if rounds > 1:
                    with act.Fori(0, rounds) as i:
                        for b in range(4):
                            act.wait_ge(slab_done, i * 4 + (g0 + b + 1))
                            af(dst(i * 4 + b), ps[b][:, :], func).then_inc(free_act, 1)
                    s = rounds * 4
                for t in range(s, count):
                    act.wait_ge(slab_done, g0 + t + 1)
                    af(dst(t), ps[t % 4][:, :], func).then_inc(free_act, 1)

            def root(dst, src, n, e=0):
                return af(dst, src, ACT.Sqrt, bias=eps[:, e:e + 1], scale=1.0 / n)

            def tiles(buf, m0=0):
                return lambda m: buf[:, bass.ds(m * 2 + m0, 2), :].rearrange("p a t -> p (a t)")

            def norm(arg):
                e, shift = arg[0], arg[1]
                pe_done.wait(act)
                root(R[:, 0, :], ps[4][:, 0:TOK], D, e).then_inc(act_done.tick(), 1)
                if shift is not None:
                    for k in range(KD):
                        dve_act.wait(act)
                        af(H[:, k, :], T[:, k, :], ACT.Identity, bias=mod[:, shift + k:shift + k + 1])\
                            .then_inc(h_ready.sem, 1)

            def ada(_):
                af(cact[:, :], V("c", 0, KD), ACT.Silu).then_inc(act_done.tick(), 1)
                act_done.own(act)
                with act.Fori(0, ADA_SLABS // 4) as i:
                    for b in range(4):
                        act.wait_ge(w_ready[b], i * 16 + 16)
                        for k in range(ADA_ACT):
                            w = ring[:, b, k * 256:(k + 1) * 256]
                            ins = af(w, w, ACT.Copy, scale=cact[:, k:k + 1])
                        ins.then_inc(ada_scaled, 1)
                act.wait_ge(con_ready, 16)
                act.wait_ge(in_ready, 48)

            def gmlp(i):
                j = i // 3
                evac(("gm_in", j), ACT.Gelu_apprx_tanh, tiles(A))
                pe_done.skip(act, 1)
                pe_done.wait(act)
                root(R[:, 0, :], ps[4][:, 256:512], GM_INNER).then_inc(act_done.tick(), 1)
                dve_act.wait(act)
                for k in range(KG):
                    ins = af(A[:, KG + k, :], A[:, KG + k, :], ACT.Identity,
                             bias=V("gm_ln_b", j * KG + k), scale=V("gm_ln_g", j * KG + k))
                    if k % 2:
                        ins.then_inc(act_pe.tick(), 1)
                        q = k // 2
                        if q >= 1:
                            copy_vt(q - 1)
                copy_vt(KG // 2 - 1)
                pe_done.skip(act, KG // 2)

            def copy_vt(q):
                pe_done.wait(act)
                af(B[:, 16 + 2 * q:18 + 2 * q, :].rearrange("p a t -> p (a t)"), ps[4 + q % 2][:, :],
                   ACT.Copy).then_inc(act_pe.tick(), 1)

            def ffn(i):
                sec = ("ff_up", i)
                g0 = first_slab[sec]
                f0 = before[sec]["dve"]

                def one(m, b, i4):
                    act.wait_ge(slab_done, i4 + (g0 + b + 1))
                    act.wait_ge(free_dve, i4 + (f0 + b))
                    for half in range(2):
                        c = m * 8 + (COL["ff_conv"] + i * KF * 8 + half * 4)
                        ins = af(C[:, b % 4, half, :], ps[b % 4][:, half * TOK:(half + 1) * TOK], ACT.Identity,
                                 bias=vec[:, bass.ds(c + 3, 1)], scale=vec[:, bass.ds(c + 2, 1)])
                    ins.then_inc(act_conv, 1)
                    act.wait_ge(free_dve, i4 + (f0 + b + 1))
                    af(C[:, b % 4, 0, :], C[:, b % 4, 0, :], ACT.Silu).then_inc(silu_done.sem, 1)

                with act.Fori(0, KF // 4) as r:
                    for b in range(4):
                        one(r * 4 + b, b, r * 4)
                for m in range(KF // 4 * 4, KF):
                    one(m, m, 0)

            def swiglu(_):
                g0 = first_slab[("sw_up", 0)]
                with act.Fori(0, KF // 4) as i:
                    for b in range(4):
                        act.wait_ge(slab_done, i * 4 + (g0 + b + 1))
                        af(C[:, b, 0, :], ps[b][:, 0:TOK], ACT.Silu).then_inc(silu_done.sem, 1)
                for m in range(KF // 4 * 4, KF):
                    act.wait_ge(slab_done, g0 + m + 1)
                    af(C[:, m % 4, 0, :], ps[m % 4][:, 0:TOK], ACT.Silu).then_inc(silu_done.sem, 1)

            def mla(_):
                dve_act.wait(act)
                af(B[:, 60, :], B[:, 60, :], ACT.Sin)
                af(B[:, 61, :], B[:, 61, :], ACT.Sin).then_inc(act_done.tick(), 1)
                evac(("mla_a", 0), ACT.Copy, tiles(A))
                pe_done.wait(act)
                root(R[:, 0, :], ps[4][:, 0:TOK], Q_RANK)
                root(R[:, 1, :], ps[4][:, 256:512], KV_RANK).then_inc(act_done.tick(), 1)
                g = first_slab[("mla_qb", 0)]
                for m in range(12):
                    if m % 4 == 3:
                        act.wait_ge(slab_done, g + m // 4 + 1)
                    else:
                        pe_done.wait(act)
                    af(B[:, 8 + 2 * m:10 + 2 * m, :].rearrange("p a t -> p (a t)"), ps[m % 4][:, :], ACT.Copy)\
                        .then_inc(free_act, 1)
                g = first_slab[("mla_kvb", 0)]
                for b in range(4):
                    pe_done.wait(act)
                    af(A[:, 8 + 2 * b:10 + 2 * b, :].rearrange("p a t -> p (a t)"), ps[b][:, :], ACT.Copy)\
                        .then_inc(free_act, 1)
                for b in range(4):
                    if b == 3:
                        act.wait_ge(slab_done, g + 1)
                    else:
                        pe_done.wait(act)
                    af(B[:, 32 + 2 * b:34 + 2 * b, :].rearrange("p a t -> p (a t)"), ps[b][:, :], ACT.Copy)\
                        .then_inc(free_act, 1)
                for h in range(HEADS):
                    s = T[:, 2 * (h % 2):2 * (h % 2) + 2, :].rearrange("p a t -> p (a t)")
                    dve_act.wait(act)
                    o = 8 * (h % 2)
                    af(s[:, 0:P], s[:, 0:P], ACT.Exp, bias=small[:, o + 2:o + 3], accum_out=small[:, o + 4:o + 5])
                    af(s[:, P:384], s[:, P:384], ACT.Exp, bias=small[:, o + 3:o + 4],
                       accum_out=small[:, o + 5:o + 6]).then_inc(act_done.tick(), 1)
                    if h + 1 < HEADS:
                        pe_done.skip(act, 1)
                    if h == 0:
                        pe_done.skip(act, 1)
                    pe_done.wait(act)
                    af(T[:, 4 + 2 * (h % 2):6 + 2 * (h % 2), :].rearrange("p a t -> p (a t)")[:, 0:384],
                       ps[2 + h % 2][:, 0:384], ACT.Copy).then_inc(act_pe.tick(), 1)
                    pe_done.wait(act)
                    af(B[:, 40 + h, :], ps[4 + h % 2][:, 0:TOK], ACT.Copy).then_inc(act_pe.tick(), 1)

            def hgrn(_):
                dve_act.wait(act)
                af(lbs[:, 0:4, :], lbs[:, 0:4, :], ACT.Exp).then_inc(act_done.tick(), 1)
                evac(("hg_in", 0), ACT.Copy, tiles(A), count=12)
                act.wait_ge(free_act, before[("hg_in", 0)]["act"] + 12)
                af(A[:, 8:16, :], A[:, 8:16, :], ACT.Sigmoid).then_inc(act_done.tick(), 1)
                g0 = first_slab[("hg_in", 0)] + 12
                iv = A[:, 24:32, :].rearrange("p (t a) c -> p t (a c)", t=2)
                for b in range(4):
                    act.wait_ge(slab_done, g0 + b + 1)
                    af(iv[:, :, b * TOK:(b + 1) * TOK], ps[b][:, :].rearrange("p (t c) -> p t c", t=2), ACT.Copy)\
                        .then_inc(free_act, 1)
                dve_act.wait(act)
                af(B[:, 8:16, :], B[:, 8:16, :], ACT.Ln).then_inc(act_done.tick(), 1)
                for _ in LEVELS:
                    dve_act.wait(act)
                    step(af(B[:, 24:32, :], B[:, 24:32, :], ACT.Abs))
                    af(B[:, 24:32, :], B[:, 24:32, :], ACT.Exp, scale=-1.0).then_inc(act_done.tick(), 1)
                pe_done.skip(act, len(LEVELS) + 1)
                for b in range(4):
                    pe_done.wait(act)
                    af(B[:, 2 * b:2 * b + 2, :].rearrange("p a t -> p (a t)"), ps[b][:, :], ACT.Copy)\
                        .then_inc(free_act, 1)
                af(B[:, 24:32, :], A[:, 16:24, :], ACT.Silu)
                pe_done.wait(act)
                for b in range(4):
                    ins = root(B[:, 16 + 2 * b:18 + 2 * b, :].rearrange("p a t -> p (a t)"), ps[4 + b][:, :], P)
                ins.then_inc(act_done.tick(), 1)

            def hybrid(i):
                evac(("hy_in", i), ACT.Copy, tiles(A))
                act.wait_ge(free_act, before[("hy_in", i)]["act"] + SLABS["hy_in"][0])
                dve_act.wait(act)
                af(B[:, 12:20, :], B[:, 4:12, :], ACT.Silu).then_inc(act_pe.tick(), 1)
                af(B[:, 40:44, :], A[:, 6:10, :], ACT.Silu)
                af(A[:, 20:22, :], A[:, 20:22, :], ACT.Sigmoid).then_inc(act_done.tick(), 1)
                dve_act.wait(act)
                step(af(B[:, 20, :], B[:, 20, :], ACT.Exp))
                af(B[:, 20, :], B[:, 20, :], ACT.Ln, bias=ones[:, 0:1])
                af(small[:, 0:1], V("a_log", i), ACT.Exp).then_inc(act_done.tick(), 1)
                pe_done.wait(act)
                af(B[:, 22:24, :].rearrange("p a t -> p (a t)"), ps[4][:, :], ACT.Copy).then_inc(act_done.tick(), 1)
                pe_done.skip(act, 2)
                for h in range(SSD_HEADS):
                    dve_act.wait(act)
                    m = T[:, 4 + 2 * (h % 2):6 + 2 * (h % 2), :].rearrange("p a t -> p (a t)")[:, 0:384]
                    af(m, m, ACT.Exp).then_inc(act_done.tick(), 1)
                pe_done.skip(act, SSD_HEADS + SSD_HEADS // 2)
                pe_done.wait(act)
                root(B[:, 52:54, :].rearrange("p a t -> p (a t)"), ps[0][:, :], 256, 1).then_inc(act_done.tick(), 1)
                pe_done.skip(act, 1)
                pe_done.wait(act)
                root(R[:, 0, :], ps[1][:, TOK:512], W_CONF, 1).then_inc(act_done.tick(), 1)
                dve_act.wait(act)
                for k in range(2):
                    ins = af(B[:, 62 + k, :], A[:, 2 + k, :], ACT.Silu, bias=V("conf_ln_b", i * 2 + k),
                             scale=V("conf_ln_g", i * 2 + k))
                ins.then_inc(act_pe.tick(), 1)

            def moe(_):
                pe_done.skip(act, 1)
                dve_act.wait(act)
                af(small[:, 40:42], small[:, 38:40], ACT.Exp).then_inc(act_done.tick(), 1)
                pe_done.wait(act)
                for n in range(4):
                    ins = af(B[:, 8 + 2 * n:10 + 2 * n, :].rearrange("p a t -> p (a t)"), ps[n][:, :], ACT.Copy)
                ins.then_inc(act_pe.tick(), 1)

                def copy_gathered():
                    for n in range(2):
                        ins = af(B[:, 16 + 2 * n:18 + 2 * n, :].rearrange("p a t -> p (a t)"), ps[6 + n][:, :],
                                 ACT.Copy)
                    ins.then_inc(act_moe, 1)

                pe_done.skip(act, 1)
                act.wait_ge(pe_moe, 1)
                copy_gathered()
                g0 = first_slab[("moe_up", 0)]
                act.wait_ge(plan_ready, 1)
                count = act.value_load(plan_i[0:1, PASSES:PASSES + 1], min_val=EXPERTS, max_val=PASSES)
                with act.Fori(0, count) as p:
                    with act.Fori(0, nu // 4) as i:
                        for b in range(4):
                            act.wait_ge(slab_done, p * SPP + i * 4 + (g0 + b + 1))
                            af(C[:, b, 0, 0:SLOTS], ps[b][:, 0:SLOTS], ACT.Silu).then_inc(silu_done.sem, 1)
                    act.wait_ge(pe_moe, p * EV_PE + 2)
                    copy_gathered()
                    act.wait_ge(pe_moe, p * EV_PE + 3)
                    af(gplace_t, ps[5][:, 256:512], ACT.Copy).then_inc(act_moe, 1)
                    for n in range(2):
                        act.wait_ge(slab_done, p * SPP + (g0 + nu + 8 * (n + 1)))
                        af(y_slot[:, n * 512:(n + 1) * 512], ps[4 + n][:, :], ACT.Copy).then_inc(act_moe, 1)

            act.wait_ge(vec_ready, 16)
            act.wait_ge(eps_ready, 2)
            run({"norm": norm, "ada": ada, "gmlp": gmlp, "ffn": ffn, "mla": mla, "hgrn": hgrn,
                 "hybrid": hybrid, "swiglu": swiglu, "moe": moe})

        @block.vector
        def _(dve):
            tt, ts, stt = nc.vector.tensor_tensor, nc.vector.tensor_scalar, nc.vector.scalar_tensor_tensor

            def step(ins):
                ins.then_inc(dve_step.tick(), 1)
                dve_step.own(dve)

            def wide(ap, n):
                return ap.rearrange("p (o t) -> p o t", o=1).to_broadcast([P, n, TOK])

            def residual(sec, per_bank, gated):
                g0 = first_slab[sec]
                for m in range(4):
                    dve.wait_ge(slab_done, g0 + per_bank * (m + 1))
                    b = m % 4 if per_bank == 1 else m % 2
                    if gated:
                        for j in range(2):
                            k = 2 * m + j
                            ins = stt(out=X[:, k, :], in0=ps[b][:, j * TOK:(j + 1) * TOK],
                                      scalar=gcol[:, k:k + 1], in1=X[:, k, :], op0=ALU.mult, op1=ALU.add)
                    else:
                        xs = X[:, 2 * m:2 * m + 2, :].rearrange("p a t -> p (a t)")
                        ins = tt(xs, xs, ps[b][:, :], ALU.add)
                    ins.then_inc(free_dve, 1)
                    dve.wait_ge(free_dve, before[sec]["dve"] + m + 1)
                    square(m)
                squared[0] = True

            squared = [False]

            def square(m):
                xs = X[:, 2 * m:2 * m + 2, :]
                tt(T[:, 2 * m:2 * m + 2, :], xs, xs, ALU.mult).then_inc(dve_pe.tick(), 1)

            def norm(arg):
                _, shift, dst, gain, scale, gate = arg
                pe_done.skip(dve, 1)
                if not squared[0]:
                    for m in range(KD // 2):
                        square(m)
                squared[0] = False
                if shift is not None:
                    stt(out=acol[:, :], in0=mod[:, scale:scale + KD], scalar=1.0, in1=vec[:, gain:gain + KD],
                        op0=ALU.add, op1=ALU.mult)
                    step(ts(gcol[:, :], mod[:, gate:gate + KD], 1.0, None, ALU.add))
                act_done.wait(dve)
                step(nc.vector.reciprocal(R[:, 0, :], R[:, 0, :]))
                for k in range(KD):
                    col = acol[:, k:k + 1] if shift is not None else vec[:, gain + k:gain + k + 1]
                    to = T if shift is not None else dst
                    ins = stt(out=to[:, k, :], in0=X[:, k, :], scalar=col, in1=R[:, 0, :],
                              op0=ALU.mult, op1=ALU.mult)
                    if shift is not None:
                        ins.then_inc(dve_act.tick(), 1)
                    elif dst is X:
                        if k == KD - 1:
                            step(ins)
                    else:
                        ins.then_inc(h_ready.sem, 1)

            def ada(_):
                act_done.wait(dve)
                cs = cact[:, ADA_ACT:KD].rearrange("p (k o) -> p k o", o=1).to_broadcast([P, KD - ADA_ACT, 256])
                with dve.Fori(0, ADA_SLABS // 4) as i:
                    for b in range(4):
                        dve.wait_ge(w_ready[b], i * 16 + 16)
                        w = ring[:, b, :].rearrange("p (k n) -> p k n", k=KD)
                        tt(w[:, ADA_ACT:KD, :], w[:, ADA_ACT:KD, :], cs, ALU.mult).then_inc(ada_own, 1)
                        dve.wait_ge(ada_own, i * 4 + (b + 1))
                        dve.wait_ge(ada_scaled, i * 4 + (b + 1))
                        nc.vector.tensor_reduce(C[:, b, 0, :], w.rearrange("p k n -> p n k"), AX_X, ALU.add)\
                            .then_inc(ada_sum, 1)
                dve.wait_ge(slab_done, ADA_SLABS)
                dve.wait_ge(con_ready, 16)
                dve.wait_ge(in_ready, 48)
                step(tt(mod[:, :], ps[4][:, 0:DEPTH * 48], V("ada_b", 0, DEPTH * 48), ALU.add))

            def gmlp(i):
                j = i // 3
                v = A[:, KG:2 * KG, :]
                ws = wsbs[:, j, 0:GM_GROUPS * P].rearrange("p (g t) -> p g t", g=GM_GROUPS)
                tt(ws, ws, tri.rearrange("p (o t) -> p o t", o=1).to_broadcast([P, GM_GROUPS, P]), ALU.mult)
                pe_done.wait(dve)
                step(ts(MU[:, :], ps[4][:, 0:TOK], 1.0 / GM_INNER, None, ALU.mult))
                step(tt(v, v, wide(MU[:, :], KG), ALU.subtract))
                tt(B[:, 0:KG, :], v, v, ALU.mult).then_inc(dve_pe.tick(), 1)
                pe_done.skip(dve, 1)
                act_done.wait(dve)
                step(nc.vector.reciprocal(R[:, 0, :], R[:, 0, :]))
                tt(v, v, wide(R[:, 0, :], KG), ALU.mult).then_inc(dve_act.tick(), 1)
                pe_done.skip(dve, KG // 2)
                for q in range(KG // 2):
                    pe_done.wait(dve)
                    t = T[:, 2 * (q % 2):2 * (q % 2) + 2, :].rearrange("p a t -> p (a t)")
                    bs = wsbs[:, j, (GM_GROUPS + q) * P:(GM_GROUPS + q + 1) * P]
                    step(tt(t.rearrange("p (r c) -> p r c", c=P), ps[6 + q % 2][:, :].rearrange("p (r c) -> p r c", c=P),
                            bs.rearrange("p (o c) -> p o c", o=1).to_broadcast([P, 4, P]), ALU.add))
                    u = A[:, 2 * q:2 * q + 2, :].rearrange("p a t -> p (a t)")
                    tt(u, u, t, ALU.mult).then_inc(dve_pe.tick(), 1)
                residual(("gm_out", j), 2, True)

            def ffn(i):
                sec = ("ff_up", i)

                def one(m, b, i4):
                    dve.wait_ge(act_conv, i4 + (i * KF + b + 1))
                    for d in (1, 2):
                        for half in range(2):
                            c = m * 8 + (COL["ff_conv"] + i * KF * 8 + half * 4)
                            o = C[:, b % 4, half, d:TOK]
                            ins = stt(out=o, in0=ps[b % 4][:, half * TOK:(half + 1) * TOK - d],
                                      scalar=vec[:, bass.ds(c + (2 - d), 1)], in1=o, op0=ALU.mult, op1=ALU.add)
                        if d == 1:
                            ins.then_inc(conv_step, 1)
                            dve.wait_ge(conv_step, i4 + (i * KF + b + 1))
                    ins.then_inc(free_dve, 1)
                    dve.wait_ge(free_dve, i4 + (before[sec]["dve"] + b + 1))
                    dve.wait_ge(silu_done.sem, i4 + (silu_done.now(dve) + b + 1))
                    tt(A[:, bass.ds(m * 1, 1), :], C[:, b % 4, 0:1, :], C[:, b % 4, 1:2, :], ALU.mult)\
                        .then_inc(g_ready.sem, 1)

                with dve.Fori(0, KF // 4) as r:
                    for b in range(4):
                        one(r * 4 + b, b, r * 4)
                for m in range(KF // 4 * 4, KF):
                    one(m, m, 0)
                silu_done.skip(dve, KF)
                residual(("ff_down", i), 4, True)

            def swiglu(_):
                s0 = silu_done.now(dve)
                with dve.Fori(0, KF // 4) as i:
                    for b in range(4):
                        dve.wait_ge(silu_done.sem, i * 4 + (s0 + b + 1))
                        tt(A[:, bass.ds(i * 4 + b, 1), :].rearrange("p a t -> p (a t)"), C[:, b, 0, :],
                           ps[b][:, TOK:512], ALU.mult).then_inc(free_dve, 1)
                for m in range(KF // 4 * 4, KF):
                    dve.wait_ge(silu_done.sem, s0 + m + 1)
                    tt(A[:, m, :], C[:, m % 4, 0, :], ps[m % 4][:, TOK:512], ALU.mult).then_inc(free_dve, 1)
                silu_done.skip(dve, KF)
                residual(("sw_down", 0), 4, False)

            def mla(_):
                ang, k, s, c = B[:, 62, :], B[:, 63, :], B[:, 60, :], B[:, 61, :]
                step(nc.vector.tensor_copy(B[:, 59, :], posi[:, :]))
                step(ts(ang, B[:, 59, :], V("inv_freq"), None, ALU.mult))
                step(ts(k, ang, float(1 / (2 * np.pi)), 12582912.0, ALU.mult, ALU.add))
                step(ts(k, k, 12582912.0, None, ALU.subtract))
                for part in (6.28125, float(np.float32(0.0019350051879882812)), float(2 * np.pi - 6.28125 - 0.0019350051879882812)):
                    step(stt(out=ang, in0=k, scalar=-part, in1=ang, op0=ALU.mult, op1=ALU.add))
                step(ts(ang, ang, float(np.float32(3.1415925)), -float(np.float32(3.1415925)), ALU.min, ALU.max))
                step(ts(k, ang, -1.0, None, ALU.mult))
                step(tt(k, k, ang, ALU.min))
                ts(c, k, float(np.pi / 2), None, ALU.add)
                ts(s, ang, V("rope_sign"), None, ALU.mult).then_inc(dve_act.tick(), 1)
                act_done.wait(dve)
                dve.wait_ge(free_act, before[("mla_a", 0)]["act"] + 3)
                tt(B[:, 0:3, :], A[:, 0:3, :], A[:, 0:3, :], ALU.mult).then_inc(dve_pe.tick(), 1)
                tt(B[:, 3, :], A[:, 3, :], c, ALU.mult)
                step(tt(B[:, 4, :], A[:, 4, :], s, ALU.mult))
                step(tt(A[:, 3, :], B[:, 3, :], B[:, 4, :], ALU.add))
                act_done.wait(dve)
                step(nc.vector.reciprocal(R[:, :, :], R[:, :, :]))
                for t in range(3):
                    g = V("q_norm", t) if t < 2 else V("kv_norm")
                    ins = stt(out=A[:, t, :], in0=A[:, t, :], scalar=g, in1=R[:, t // 2, :],
                              op0=ALU.mult, op1=ALU.mult)
                ins.then_inc(dve_pe.tick(), 1)
                dve.wait_ge(free_act, before[("mla_qb", 0)]["act"] + 12)
                tt(B[:, 16:24, :], B[:, 16:24, :], wide(c, 8), ALU.mult)
                step(tt(B[:, 24:32, :], B[:, 24:32, :], wide(s, 8), ALU.mult))
                tt(B[:, 16:24, :], B[:, 16:24, :], B[:, 24:32, :], ALU.add).then_inc(dve_pe.tick(), 1)
                pe_done.skip(dve, 1 + 9 + 7)
                for h in range(HEADS):
                    if h < 1:
                        pe_done.wait(dve)
                    o = 8 * (h % 2)
                    s_ = T[:, 2 * (h % 2):2 * (h % 2) + 2, :].rearrange("p a t -> p (a t)")
                    b = ps[h % 2]
                    for lo in (0, TOK):
                        stt(out=s_[:, lo:lo + P], in0=b[:, lo:lo + P], scalar=ATT_SCALE, in1=negm,
                            op0=ALU.mult, op1=ALU.add)
                    step(ts(s_[:, P:TOK], b[:, P:TOK], ATT_SCALE, None, ALU.mult))
                    nc.vector.tensor_reduce(small[:, o:o + 1], s_[:, 0:P], AX_X, ALU.max)
                    step(nc.vector.tensor_reduce(small[:, o + 1:o + 2], s_[:, P:384], AX_X, ALU.max))
                    ts(small[:, o + 2:o + 4], small[:, o:o + 2], -1.0, None, ALU.mult).then_inc(dve_act.tick(), 1)
                    act_done.wait(dve)
                    step(nc.vector.reciprocal(small[:, o + 6:o + 8], small[:, o + 4:o + 6]))
                    ts(s_[:, 0:P], s_[:, 0:P], small[:, o + 6:o + 7], None, ALU.mult)
                    ts(s_[:, P:384], s_[:, P:384], small[:, o + 7:o + 8], None, ALU.mult).then_inc(dve_pe.tick(), 1)
                    if h + 1 < HEADS:
                        pe_done.wait(dve)
                    pe_done.skip(dve, 2)
                residual(("mla_o", 0), 1, True)

            def hgrn(_):
                lb = lbs[:, 0:4, :]
                src = vec[:, COL["hg_lb"]:COL["hg_lb"] + DEPTH * KD].rearrange("p (d k) -> p d k", d=DEPTH)
                step(tt(lbs[:, 4:6, :], src[:, 0:2, :], src[:, 2:4, :], ALU.max))
                step(tt(lbs[:, 4, :], lbs[:, 4, :], lbs[:, 5, :], ALU.max))
                tt(lb, src, lbs[:, 4:5, :].to_broadcast([P, 4, KD]), ALU.subtract).then_inc(dve_act.tick(), 1)
                act_done.wait(dve)
                step(tt(lbs[:, 4:6, :], lbs[:, 0:2, :], lbs[:, 2:4, :], ALU.add))
                step(tt(lbs[:, 4, :], lbs[:, 4, :], lbs[:, 5, :], ALU.add))
                step(nc.vector.reciprocal(lbs[:, 4, :], lbs[:, 4, :]))
                step(tt(lbs[:, 5, :], lbs[:, 1, :], lbs[:, 2, :], ALU.add))
                step(tt(lbs[:, 0, :], lbs[:, 5, :], lbs[:, 4, :], ALU.mult))
                step(ts(lbs[:, 1, :], lbs[:, 0, :], -1.0, 1.0, ALU.mult, ALU.add))
                act_done.wait(dve)
                for k in range(KD):
                    ins = ts(B[:, 8 + k, :], A[:, 8 + k, :], lbs[:, 1, k:k + 1], lbs[:, 0, k:k + 1],
                             ALU.mult, ALU.add)
                step(ins)
                ts(B[:, 0:8, :], B[:, 8:16, :], -1.0, 1.0, ALU.mult, ALU.add).then_inc(dve_act.tick(), 1)
                act_done.wait(dve)
                for k in range(KD):
                    ins = nc.vector.tensor_tensor_scan(B[:, 16 + k, :], ones_wide, B[:, 8 + k, :], 0.0,
                                                       ALU.mult, ALU.add)
                step(ins)
                att = B[:, 48:60, :].rearrange("p a c -> p (a c)").rearrange("p (h r c) -> p h r c", h=HEADS, r=3)
                bc = B[:, 16:24, :].rearrange("p a c -> p (a c)")
                dd = B[:, 24:32, :].rearrange("p a c -> p (a c)")

                def gather(n):
                    pe_done.wait(dve)
                    if n == 0:
                        for b in range(2):
                            ins = nc.vector.tensor_copy(att[:, 4 * b:4 * b + 4, 1, :],
                                                        ps[4 + b][:, :].rearrange("p (h c) -> p h c", c=P))
                        ins.then_inc(dve_pe.tick(), 1)
                        return
                    m = con[:, CONST["mask"] + (n - 1) * P:CONST["mask"] + n * P]
                    m = m.rearrange("p (o c) -> p o c", o=1).to_broadcast([P, 4, P])
                    for b in range(4):
                        ins = tt(T[:, 2 * b:2 * b + 2, :].rearrange("p a (r c) -> p (a r) c", c=P),
                                 ps[4 + b][:, :].rearrange("p (r c) -> p r c", c=P), m, ALU.mult)
                    ins.then_inc(dve_pe.tick(), 1)
                    dve_pe.own(dve)
                    t4 = T[:, :, :].rearrange("p h (r c) -> p h r c", c=P)
                    if n == 1:
                        step(nc.vector.tensor_copy(att[:, :, 0:3:2, :], t4))
                    else:
                        ins = tt(att[:, :, 0:3:2, :], att[:, :, 0:3:2, :], t4, ALU.add)
                        if n == len(LEVELS):
                            ins.then_inc(dve_pe.tick(), 1)
                        else:
                            step(ins)

                for n, L in enumerate(LEVELS):
                    g = 8 * TOK // (2 * L)
                    bv = bc.rearrange("p (g l) -> p g l", l=2 * L)
                    if n:
                        dve_pe.own(dve)
                    tt(dd.rearrange("p (g l) -> p g l", l=2 * L), bv,
                       bv[:, :, L - 1:L].to_broadcast([P, g, 2 * L]), ALU.subtract).then_inc(dve_act.tick(), 1)
                    if n:
                        gather(n - 1)
                    act_done.wait(dve)
                    tt(B[:, 32:40, :], A[:, 0:8, :], B[:, 24:32, :], ALU.mult)
                    tt(B[:, 40:48, :], B[:, 0:8, :], B[:, 24:32, :], ALU.mult).then_inc(dve_pe.tick(), 1)
                gather(len(LEVELS) - 1)
                gather(len(LEVELS))
                dve.wait_ge(free_act, before[("hg_in", 0)]["act"] + 20)
                tt(B[:, 8:16, :], B[:, 0:8, :], B[:, 0:8, :], ALU.mult).then_inc(dve_pe.tick(), 1)
                pe_done.skip(dve, 5)
                act_done.wait(dve)
                step(nc.vector.reciprocal(B[:, 16:24, :], B[:, 16:24, :]))
                step(stt(out=B[:, 0:8, :], in0=B[:, 0:8, :], scalar=V("hg_norm"), in1=B[:, 16:24, :],
                         op0=ALU.mult, op1=ALU.mult))
                tt(B[:, 32:40, :], B[:, 0:8, :], B[:, 24:32, :], ALU.mult).then_inc(dve_pe.tick(), 1)
                residual(("hg_o", 0), 1, True)

            def causal_conv(dst, src, n, col, taps, bias):
                for k in range(n):
                    w = col(k)
                    if bias:
                        ins = ts(dst(k), src(k), vec[:, w + taps - 1:w + taps], vec[:, w + taps:w + taps + 1],
                                 ALU.mult, ALU.add)
                    else:
                        ins = ts(dst(k), src(k), vec[:, w + taps - 1:w + taps], None, ALU.mult)
                for d in range(1, taps):
                    step(ins)
                    for k in range(n):
                        c = col(k) + taps - 1 - d
                        ins = stt(out=dst(k)[:, d:TOK], in0=src(k)[:, 0:TOK - d], scalar=vec[:, c:c + 1],
                                  in1=dst(k)[:, d:TOK], op0=ALU.mult, op1=ALU.add)
                return ins

            def hybrid(i):
                dve.wait_ge(free_act, before[("hy_in", i)]["act"] + 9)
                causal_conv(lambda k: B[:, 4 + k, :], lambda k: A[:, 10 + k, :], 8,
                            lambda k: COL["conv_ssd"] + (i * 8 + k) * 5, 4, True).then_inc(dve_act.tick(), 1)
                step(tt(B[:, 0:2, :], A[:, 2:4, :], A[:, 4:6, :], ALU.mult))
                step(causal_conv(lambda k: B[:, 2 + k, :], lambda k: B[:, k, :], 2,
                                 lambda k: COL["conv_a"] + (i * 2 + k) * 3, 3, False))
                tt(B[:, 56:58, :], A[:, 0:2, :], B[:, 2:4, :], ALU.mult)
                dve.wait_ge(free_act, before[("hy_in", i)]["act"] + SLABS["hy_in"][0])
                step(ts(B[:, 22, :], A[:, 22, :], V("dt_bias", i), None, ALU.add))
                step(ts(B[:, 21, :], B[:, 22, :], -1.0, None, ALU.mult))
                tt(B[:, 20, :], B[:, 21, :], B[:, 22, :], ALU.min).then_inc(dve_act.tick(), 1)
                step(ts(B[:, 22, :], B[:, 22, :], 0.0, None, ALU.max))
                nc.vector.memset(B[:, 24:32, :], 0.0)
                act_done.wait(dve, 2)
                step(tt(B[:, 20, :], B[:, 20, :], B[:, 22, :], ALU.add))
                step(ts(B[:, 23, :], B[:, 20, :], small[:, 0:1], -1.0, ALU.mult, ALU.mult))
                nc.vector.tensor_tensor_scan(B[:, 21, :], ones_wide, B[:, 23, :], 0.0, ALU.mult, ALU.add)\
                    .then_inc(dve_pe.tick(), 1)
                act_done.wait(dve)
                pe_done.wait(dve, 2)
                cols = B[:, 22:24, :].rearrange("p a (r c) -> p (a r) c", c=P)
                for h in range(SSD_HEADS):
                    for t in range(2):
                        o = t * P + (h % 2) * 64
                        ins = ts(B[:, 24 + h, o:o + 64], ps[5 + t][:, h * 64:(h + 1) * 64],
                                 cols[:, t, h:h + 1], None, ALU.mult)
                ins.then_inc(dve_pe.tick(), 1)
                pe_done.wait(dve)
                cb = B[:, 32:35, :].rearrange("p a c -> p (a c)").rearrange("p (g c) -> p g c", g=2)
                for g in range(SSD_GROUPS):
                    tt(cb[:, g, 0:P], ps[2 + g][:, 0:P], tri, ALU.mult)
                    nc.vector.tensor_copy(cb[:, g, P:TOK], ps[2 + g][:, P:TOK])
                    ins = tt(cb[:, g, TOK:384], ps[2 + g][:, TOK:384], tri, ALU.mult)
                step(ins)
                step(tt(A[:, 18:20, :], A[:, 18:20, :], A[:, 20:22, :], ALU.mult))

                def conf_taps(first, end):
                    for d in range(first, min(end, CONF_KERNEL)):
                        for k in range(2):
                            c = COL["conf_conv"] + (i * 2 + k) * 32 + CONF_KERNEL - 1 - d
                            if d == 0:
                                ins = ts(A[:, 2 + k, :], A[:, 18 + k, :], vec[:, c:c + 1], vec[:, c + 1:c + 2],
                                         ALU.mult, ALU.add)
                            else:
                                ins = stt(out=A[:, 2 + k, d:TOK], in0=A[:, 18 + k, 0:TOK - d],
                                          scalar=vec[:, c:c + 1], in1=A[:, 2 + k, d:TOK],
                                          op0=ALU.mult, op1=ALU.add)
                        if d < CONF_KERNEL - 1:
                            step(ins)
                    return ins

                for h in range(SSD_HEADS):
                    pe_done.wait(dve, 2 if h >= 3 and h % 2 else 1)
                    m = T[:, 4 + 2 * (h % 2):6 + 2 * (h % 2), :].rearrange("p a t -> p (a t)")[:, 0:384]
                    ts(m[:, 0:TOK], ps[h % 2][:, 0:TOK], cols[:, 2, h:h + 1], 0.0, ALU.subtract, ALU.min)
                    ts(m[:, TOK:384], ps[h % 2][:, P:TOK], cols[:, 3, h:h + 1], 0.0, ALU.subtract, ALU.min)\
                        .then_inc(dve_act.tick(), 1)
                    conf_taps(4 * h, min(4 * h + 4, CONF_KERNEL - 1))
                    act_done.wait(dve)
                    tt(m, m, cb[:, h // 4, :], ALU.mult).then_inc(dve_pe.tick(), 1)
                pe_done.wait(dve)
                for p in range(4):
                    ins = stt(out=B[:, 36 + p, :], in0=B[:, 12 + p, :], scalar=V("d_skip", i * 4 + p),
                              in1=ps[4 + p][:, 0:TOK], op0=ALU.mult, op1=ALU.add)
                step(ins)
                step(tt(B[:, 44:48, :], B[:, 36:40, :], B[:, 40:44, :], ALU.mult))
                tt(B[:, 48:52, :], B[:, 44:48, :], B[:, 44:48, :], ALU.mult).then_inc(dve_pe.tick(), 1)
                conf_taps(CONF_KERNEL - 1, CONF_KERNEL).then_inc(dve_pe.tick(), 1)
                pe_done.wait(dve, 2)
                step(ts(MU[:, :], ps[1][:, 0:TOK], 1.0 / W_CONF, None, ALU.mult))
                step(tt(A[:, 2:4, :], A[:, 2:4, :], wide(MU[:, :], 2), ALU.subtract))
                tt(A[:, 4:6, :], A[:, 2:4, :], A[:, 2:4, :], ALU.mult).then_inc(dve_pe.tick(), 1)
                act_done.wait(dve)
                step(nc.vector.reciprocal(B[:, 52:54, :], B[:, 52:54, :]))
                for p in range(4):
                    ins = stt(out=B[:, 58 + p, :], in0=B[:, 44 + p, :], scalar=V("ssd_norm", i * 4 + p),
                              in1=B[:, 52 + p // 2, :], op0=ALU.mult, op1=ALU.mult)
                ins.then_inc(dve_pe.tick(), 1)
                pe_done.skip(dve, 1)
                act_done.wait(dve)
                step(nc.vector.reciprocal(R[:, 0, :], R[:, 0, :]))
                tt(A[:, 2:4, :], A[:, 2:4, :], wide(R[:, 0, :], 2), ALU.mult).then_inc(dve_act.tick(), 1)
                residual(("hy_out", i), 1, False)

            def moe(_):
                lg, eq, one, two, l2, gt = [rt[:, n, :, :] for n in range(6)]
                m1, m2, pick = small[:, 32:34], small[:, 34:36], small[:, 36:38]
                prior = con[:, CONST["prior"]:CONST["prior"] + EXPERTS]
                prior = prior.rearrange("p (o e) -> p o e", o=1).to_broadcast([P, 2, EXPERTS])

                def each(col):
                    return col.rearrange("p (t o) -> p t o", o=1).to_broadcast([P, 2, EXPERTS])

                def best(hot, logits, top):
                    step(nc.vector.tensor_reduce(top, logits, AX_X, ALU.max))
                    step(tt(eq, logits, each(top), ALU.is_equal))
                    step(tt(eq, eq, prior, ALU.mult))
                    step(nc.vector.tensor_reduce(pick, eq, AX_X, ALU.max))
                    step(tt(hot, eq, each(pick), ALU.is_equal))

                step(nc.vector.memset(passes[:, :, :, :], 0.0))
                pe_done.wait(dve)
                step(nc.vector.tensor_copy(lg, ps[4][:, 0:16].rearrange("p (t e) -> p t e", t=2)))
                best(one, lg, m1)
                step(stt(out=l2, in0=one, scalar=NEG, in1=lg, op0=ALU.mult, op1=ALU.add))
                best(two, l2, m2)
                chosen, place_no, gate = [passes[:, n, :, 0:EXPERTS] for n in range(3)]
                tt(chosen, one, two, ALU.add).then_inc(dve_pe.tick(), 1)
                tt(small[:, 38:40], m2, m1, ALU.subtract).then_inc(dve_act.tick(), 1)
                act_done.wait(dve)
                step(ts(small[:, 42:44], small[:, 40:42], 1.0, None, ALU.add))
                step(nc.vector.reciprocal(small[:, 42:44], small[:, 42:44]))
                step(tt(small[:, 44:46], small[:, 40:42], small[:, 42:44], ALU.mult))
                tt(one, one, each(small[:, 42:44]), ALU.mult)
                step(tt(two, two, each(small[:, 44:46]), ALU.mult))
                step(tt(gate, one, two, ALU.add))
                pe_done.wait(dve, 2)
                ts(place_no, ps[6][:, 0:16].rearrange("p (t e) -> p t e", t=2), 1.0, None, ALU.subtract)
                over, nth, hot = l2[:, 0, :], l2[:, 1, :], eq[:, 0, :]
                step(ts(over, ps[6][:, 16:24], SLOTS + 0.5, None, ALU.is_gt))
                step(nc.vector.tensor_tensor_scan(nth, ones[:, 0:EXPERTS], over, 0.0, ALU.mult, ALU.add))
                experts = con[:, CONST["expert"]:CONST["expert"] + EXPERTS]
                nc.vector.tensor_copy(plan[:, 0:EXPERTS], experts)
                ts(plan[:, PASSES:PASSES + 1], nth[:, EXPERTS - 1:EXPERTS], float(EXPERTS), None, ALU.add)
                for j in range(PASSES - EXPERTS):
                    step(stt(out=hot, in0=nth, scalar=float(j + 1), in1=over, op0=ALU.is_equal, op1=ALU.mult))
                    o = EXPERTS + j
                    for n in range(3):
                        step(tt(lg, passes[:, n, :, 0:EXPERTS],
                                hot.rearrange("p (t e) -> p t e", t=1).to_broadcast([P, 2, EXPERTS]), ALU.mult))
                        step(nc.vector.tensor_reduce(passes[:, n, :, o:o + 1].rearrange("p t o -> p (t o)"), lg,
                                                     AX_X, ALU.add))
                    ts(passes[:, 1, :, o:o + 1], passes[:, 1, :, o:o + 1], float(SLOTS), None, ALU.subtract)
                    step(tt(lg[:, 0, :], experts, hot, ALU.mult))
                    step(nc.vector.tensor_reduce(plan[:, o:o + 1], lg[:, 0, :], AX_X, ALU.add))
                nc.vector.tensor_copy(plan_i[:, :], plan[:, :]).then_inc(plan_ready, 1)
                iota = con[:, CONST["iota"]:CONST["iota"] + SLOTS]

                def put(dst, what, at):
                    for t in range(2):
                        ins = ts(dst[:, t * SLOTS:(t + 1) * SLOTS], iota, passes[:, 1, t, at],
                                 passes[:, what, t, at], ALU.is_equal, ALU.mult)
                    return ins

                put(place, 0, slice(0, 1)).then_inc(dve_moe, 1)
                f0, s0 = before[("moe_up", 0)]["dve"], silu_done.now(dve)
                dve.wait_ge(plan_ready, 1)
                count = dve.value_load(plan_i[0:1, PASSES:PASSES + 1], min_val=EXPERTS, max_val=PASSES)
                with dve.Fori(0, count) as p:
                    dve.wait_ge(pe_moe, p * EV_PE + 1)
                    put(gplace, 2, bass.ds(p, 1))
                    put(place, 0, bass.ds(p + 1, 1)).then_inc(dve_moe, 1)
                    with dve.Fori(0, nu // 4) as i:
                        for b in range(4):
                            dve.wait_ge(silu_done.sem, p * nu + i * 4 + (s0 + b + 1))
                            tt(A[:, bass.ds(i * 4 + b, 1), 0:SLOTS].rearrange("p a t -> p (a t)"),
                               C[:, b, 0, 0:SLOTS], ps[b][:, SLOTS:2 * SLOTS], ALU.mult).then_inc(free_dve, 1)
                    dve.wait_ge(dve_add, p * EV_ADD + 1)
                    for m in range(4):
                        dve.wait_ge(pe_moe, p * EV_PE + 4 + m)
                        xs = X[:, 2 * m:2 * m + 2, :].rearrange("p a t -> p (a t)")
                        tt(xs, xs, ps[6 + m % 2][:, :], ALU.add).then_inc(dve_add, 1)
                dve.wait_ge(dve_add, count * EV_ADD + 1)

            nc.vector.memset(eps[:, 0:1], EPS).then_inc(eps_ready, 1)
            nc.vector.memset(eps[:, 1:2], EPS_2).then_inc(eps_ready, 1)
            nc.vector.memset(small[:, 47:48], 0.0).then_inc(dve_add, 1)
            for b in range(CREDIT):
                nc.vector.memset(small[:, 48 + b:49 + b], 0.0).then_inc(free_act, 1)
                nc.vector.memset(small[:, 56 + b:57 + b], 0.0).then_inc(free_dve, 1)
            dve.wait_ge(vec_ready, 16)
            run({"norm": norm, "ada": ada, "gmlp": gmlp, "ffn": ffn, "mla": mla, "hgrn": hgrn,
                 "hybrid": hybrid, "swiglu": swiglu, "moe": moe})


def columns(v):
    v = np.ascontiguousarray(v).reshape(-1, P)
    return v.T


def pairs(w):
    n = w.shape[1] // 256
    return w.reshape(KD, P, n, 256).transpose(2, 1, 0, 3).reshape(n, P, KD * 256)


def gate_and_value(w):
    k, n = w.shape
    return w.reshape(k, 2, n // 256, P).transpose(0, 2, 1, 3).reshape(k, n)


def deep(w, tiles):
    parts = w.shape[0] // P // tiles
    return w.reshape(parts, tiles, P, 8, P).transpose(3, 0, 2, 1, 4).reshape(8 * parts, P, tiles * P)


def lay_out(v):
    f = {k: np.asarray(a) for k, a in v.items()}

    def zeros(*shape):
        return np.zeros(shape, np.float32)

    a = {}
    a["w_ada"] = np.concatenate([pairs(w) for w in f["ada_w"]])
    a["w_gm_in"] = np.concatenate([pairs(w) for w in f["gm_w_in"]])
    a["w_gm_out"] = np.concatenate([deep(w, 16) for w in f["gm_w_out"]])
    w = f["mla_w_a"][0]
    r1, r2, z = w[:, 384:416], w[:, 416:448], zeros(D, 64)
    a["w_mla_a"] = pairs(np.concatenate([w[:, :384], r1, r2, z, r2, r1, z, zeros(D, P)], 1))
    w = f["mla_w_qb"][0].reshape(Q_RANK, HEADS, NOPE + ROPE)
    r1, r2, z = w[:, :, 128:160], w[:, :, 160:192], zeros(Q_RANK, HEADS, 64)
    w = np.stack([w[:, :, :128], np.concatenate([r1, r2, z], 2), np.concatenate([r2, r1, z], 2)], 1)
    a["w_mla_qb"] = w.reshape(2, P, 3, 4, 2, P).transpose(2, 1, 3, 0, 4, 5).reshape(3, P, 16 * P)
    w = f["mla_w_kvb"][0].reshape(KV_RANK, HEADS, 2, 128).transpose(0, 2, 1, 3)
    a["w_mla_kvb"] = w.reshape(1, P, 16 * P)
    a["w_mla_o"] = pairs(f["mla_w_o"][0])
    w = f["hg_w_in"][0]
    a["w_hg_in"] = pairs(np.concatenate([w[:, :2048], w[:, 3072:], w[:, 2048:3072]], 1))
    a["w_hg_o"] = pairs(f["hg_w_o"][0])
    a["w_ff_up"] = np.concatenate([pairs(gate_and_value(w)) for w in f["ff_w_up"]])
    a["w_ff_down"] = np.concatenate([deep(w, KF // 2) for w in f["ff_w_down"]])
    hy = []
    for w in f["w_in_2"]:
        hy.append(pairs(np.concatenate([w[:, :2304], w[:, 2312:], w[:, 2304:2312], zeros(D, 120), zeros(D, P)], 1)))
    a["w_hy_in"] = np.concatenate(hy)
    a["w_hy_out"] = np.concatenate([pairs(w) for w in f["w_out_2"]])
    a["w_sw_up"] = pairs(gate_and_value(np.concatenate([f["ffn_w_gate_2"][0], f["ffn_w_up_2"][0]], 1)))
    a["w_sw_down"] = deep(f["ffn_w_down_2"][0], KF // 2)
    a["w_moe_up"] = np.concatenate([pairs(gate_and_value(np.concatenate([g, u], 1)))
                                    for g, u in zip(f["moe_w_gate_2"][0], f["moe_w_up_2"][0])])
    a["w_moe_down"] = np.concatenate([w.reshape(4, KE // 4, P, 4, 256).transpose(3, 0, 2, 1, 4)
                                      .reshape(16, P, KE // 4 * 256) for w in f["moe_w_down_2"][0]])

    freq = (ROPE_THETA ** (-np.arange(0, ROPE, 2, dtype=np.float32) / ROPE)).astype(np.float32)
    half = ROPE // 2

    def taps(w, b, tiles):
        rows = [w] if b is None else [w, b[None]]
        w = np.concatenate(rows)
        return w.reshape(w.shape[0], tiles, P).transpose(2, 1, 0).reshape(P, -1)

    def padded(x):
        return np.concatenate([x, zeros(P - SSD_HEADS)]).reshape(P, 1)

    ff = []
    for w, b in zip(f["ff_conv_w"], f["ff_conv_b"]):
        w = np.concatenate([w, b[None]]).reshape(4, 2, KF, P).transpose(3, 2, 1, 0)
        ff.append(w.reshape(P, KF * 8))
    vectors = {
        "c": columns(f["c"]), "ada_b": columns(f["ada_b"]), "mix_g": columns(f["mix_norm_g"]),
        "ffn_g": columns(f["ffn_norm_g"]), "gm_ln_g": columns(f["gm_ln_g"]), "gm_ln_b": columns(f["gm_ln_b"]),
        "q_norm": columns(f["mla_q_norm_g"]), "kv_norm": columns(f["mla_kv_norm_g"]),
        "hg_lb": columns(f["hg_lb"]), "hg_norm": columns(f["hg_norm_g"]), "ff_conv": np.concatenate(ff, 1),
        "final_g": columns(f["final_g"]), "norm_mix_2": columns(f["norm_mix_2"]),
        "conv_a": np.concatenate([taps(w, None, 2) for w in f["conv_a_w_2"]], 1),
        "conv_ssd": np.concatenate([taps(w, b, 8) for w, b in zip(f["conv_ssd_w_2"], f["conv_ssd_b_2"])], 1),
        "dt_bias": np.concatenate([padded(x) for x in f["dt_bias_2"]], 1),
        "a_log": np.concatenate([padded(x) for x in f["a_log_2"]], 1),
        "d_skip": columns(np.repeat(f["d_skip_2"], 64, axis=1)),
        "ssd_norm": columns(f["ssd_norm_w_2"]),
        "conf_conv": np.concatenate([taps(w, b, 2) for w, b in zip(f["conv_conf_w_2"], f["conv_conf_b_2"])], 1),
        "conf_ln_g": columns(f["conf_ln_g_2"]), "conf_ln_b": columns(f["conf_ln_b_2"]),
        "norm_ffn_2": columns(f["norm_ffn_2"]), "norm_final_2": columns(f["norm_final_2"]),
        "inv_freq": np.concatenate([freq, freq, zeros(64)]).reshape(P, 1),
        "rope_sign": np.concatenate([-np.ones(half), np.ones(half), np.zeros(64)]).astype(np.float32).reshape(P, 1),
        "router": f["moe_router_2"][0].reshape(KD, P, EXPERTS).transpose(1, 0, 2).reshape(P, KD * EXPERTS),
    }
    assert [(n, COL[n]) for n in vectors] == list(COL.items())
    a["vectors"] = np.concatenate(list(vectors.values()), 1)

    s, t = np.arange(P)[:, None], np.arange(P)[None, :]
    blocks = [(s // (2 * L) == t // (2 * L)) & (s // L % 2 == 0) & (t // L % 2 == 1) for L in LEVELS[1:]]
    blocks += [s == t, s == t, s <= t, np.where(t <= s, 0.0, NEG), np.ones((P, TOK))]
    blocks += [np.broadcast_to(s == e, (P, P)) for e in range(8)]
    blocks += [np.broadcast_to(np.arange(P), (P, P))]
    blocks += [np.broadcast_to(EXPERTS - np.arange(EXPERTS), (P, EXPERTS))]
    blocks += [np.broadcast_to(np.arange(EXPERTS), (P, EXPERTS))]
    a["constants"] = np.concatenate([b.astype(np.float32) for b in blocks], 1)

    ws = f["gm_w_s"].transpose(0, 3, 1, 2).reshape(2, P, GM_GROUPS * P)
    bs = np.broadcast_to(f["gm_b_s"].reshape(2, 1, GM_GROUPS * P), (2, P, GM_GROUPS * P))
    a["spatial"] = np.concatenate([ws, bs], 2).transpose(1, 0, 2)
    a["x"] = f["x"][0].reshape(TOK, KD, P).transpose(2, 1, 0)
    a["positions"] = np.broadcast_to(f["positions"][0], (P, TOK))
    return {k: np.ascontiguousarray(x) for k, x in a.items()}


def kernel(**inputs):
    import numpy as _np
    import concourse.bacc as _bacc
    from concourse import mybir as _mybir
    from concourse.bass_utils import run_bass_kernel_spmd as _run

    nc = _bacc.Bacc("TRN2", target_bir_lowering=False, num_devices=1)
    arrays = lay_out(inputs)
    ins = {k: nc.dram_tensor(k, x.shape, _mybir.dt.from_np(x.dtype), kind="ExternalInput").ap()
           for k, x in arrays.items()}
    out = nc.dram_tensor("out", (P, KD, TOK), _mybir.dt.float32, kind="ExternalOutput").ap()
    build(nc, ins, out)
    r = _run(nc, [arrays], core_ids=[0])
    got = r.results[0]["out"]
    return _np.ascontiguousarray(got.transpose(2, 1, 0)).reshape(1, TOK, D)
```
